# Optimizing a Trainium2 kernel written in Bass

```python
import jax, jax.numpy as jnp
from jax import lax
import numpy as np

D_MODEL = 1024
BATCH = 1
SEQ = 256
DEPTH = 2

HEAD_DIM = 64
BLOCK = 128
SWA_Q_HEADS = 8
SWA_KV_HEADS = 2
SWA_GROUP = SWA_Q_HEADS // SWA_KV_HEADS
SWA_WINDOW = 128
SB_HEADS = 8
ROPE_THETA = 10000.0
SWA_WIDTH = SWA_Q_HEADS * HEAD_DIM
SWA_KV_WIDTH = SWA_KV_HEADS * HEAD_DIM
SB_WIDTH = SB_HEADS * HEAD_DIM
N_BRANCHES = 2
OFF_K_SWA = SWA_WIDTH
OFF_V_SWA = OFF_K_SWA + SWA_KV_WIDTH
OFF_Q_SB = OFF_V_SWA + SWA_KV_WIDTH
OFF_K_SB = OFF_Q_SB + SB_WIDTH
OFF_V_SB = OFF_K_SB + SB_WIDTH
OFF_GATE_SWA = OFF_V_SB + SB_WIDTH
OFF_GATE_SB = OFF_GATE_SWA + D_MODEL
IN_COLS = OFF_GATE_SB + D_MODEL
IN_SPLITS = (OFF_K_SWA, OFF_V_SWA, OFF_Q_SB, OFF_K_SB, OFF_V_SB, OFF_GATE_SWA, OFF_GATE_SB)
PEER_HEADS = 8
PEER_NKEYS = 128
PEER_EXPERTS = PEER_NKEYS * PEER_NKEYS
PEER_TOPK = 16
PEER_QDIM = 256
PEER_HALF = PEER_QDIM // 2
PEER_CHUNK = 128
N_MOD = 6
NORM_EPS = 1e-6
NEG_INF = -1e30

kernel_name = "hybrid_swa_stickbreak_peer_adaln"

def rms_norm(x, g):
    x32 = x.astype(jnp.float32)
    y = x32 * lax.rsqrt(jnp.mean(x32 * x32, axis=-1, keepdims=True) + NORM_EPS)
    return (y * g.astype(jnp.float32)).astype(x.dtype)

def apply_rope(x, positions):
    dh = x.shape[-1]
    half = dh // 2
    inv_freq = jnp.power(ROPE_THETA, -jnp.arange(half, dtype=jnp.float32) * (2.0 / dh))
    ang = positions.astype(jnp.float32)[..., None] * inv_freq
    cos = jnp.cos(ang)[:, :, None, :]
    sin = jnp.sin(ang)[:, :, None, :]
    x32 = x.astype(jnp.float32)
    x1, x2 = x32[..., :half], x32[..., half:]
    return jnp.concatenate([x1 * cos - x2 * sin, x2 * cos + x1 * sin], axis=-1).astype(x.dtype)

def sliding_window_attention(q, k, v, sinks):
    B, S = q.shape[0], q.shape[1]
    nb = S // BLOCK
    qb = q.reshape(B, nb, BLOCK, SWA_KV_HEADS, SWA_GROUP, HEAD_DIM)

    def banded(t):
        tb = t.reshape(B, nb, BLOCK, SWA_KV_HEADS, HEAD_DIM)
        prev = jnp.pad(tb, ((0, 0), (1, 0), (0, 0), (0, 0), (0, 0)))[:, :-1]
        return jnp.concatenate([prev, tb], axis=2)

    kw, vw = banded(k), banded(v)
    scores = jnp.einsum('bnqhgd,bnkhd->bnhgqk', qb, kw).astype(jnp.float32) * (HEAD_DIM ** -0.5)
    qi = jnp.arange(BLOCK)[:, None] + BLOCK
    kj = jnp.arange(2 * BLOCK)[None, :]
    diff = qi - kj
    in_window = (diff >= 0) & (diff < SWA_WINDOW)
    key_abs = jnp.arange(nb)[:, None] * BLOCK - BLOCK + kj
    valid = in_window[None] & (key_abs >= 0)[:, None, :]
    scores = jnp.where(valid[None, :, None, None], scores, NEG_INF)
    sink = jnp.broadcast_to(
        sinks.astype(jnp.float32).reshape(1, 1, SWA_KV_HEADS, SWA_GROUP, 1, 1),
        scores.shape[:-1] + (1,))
    probs = jax.nn.softmax(jnp.concatenate([scores, sink], axis=-1), axis=-1)[..., :-1]
    out = jnp.einsum('bnhgqk,bnkhd->bnqhgd', probs.astype(v.dtype), vw)
    return out.reshape(B, S, SWA_WIDTH)

def stick_breaking_attention(q, k, v):
    B, S = q.shape[0], q.shape[1]
    nb = S // BLOCK
    qb = q.reshape(B, nb, BLOCK, SB_HEADS, HEAD_DIM).transpose(1, 0, 3, 2, 4)
    kt = k.transpose(0, 2, 1, 3)
    vt = v.transpose(0, 2, 1, 3)
    kpos = jnp.arange(S)

    def one_block(args):
        q_blk, blk = args
        z = jnp.einsum('bhqd,bhkd->bhqk', q_blk, kt).astype(jnp.float32) * (HEAD_DIM ** -0.5)
        qpos = blk * BLOCK + jnp.arange(BLOCK)
        strict = kpos[None, :] < qpos[:, None]
        log_1m = jnp.where(strict, jax.nn.log_sigmoid(-z), 0.0)
        between = lax.cumsum(log_1m, axis=3, reverse=True) - log_1m
        attn = jnp.where(strict, jnp.exp(jax.nn.log_sigmoid(z) + between), 0.0)
        return jnp.einsum('bhqk,bhkd->bhqd', attn.astype(vt.dtype), vt)

    out = lax.map(one_block, (qb, jnp.arange(nb)))
    return out.transpose(1, 0, 3, 2, 4).reshape(B, S, SB_WIDTH)

def peer_ffn(h, w_q, sub_keys, u, v):
    B, S, D = h.shape
    q = (h @ w_q).reshape(B, S, PEER_HEADS, 2, PEER_HALF)
    sk = jnp.einsum('bshpd,hpnd->bshpn', q, sub_keys).astype(jnp.float32)
    top_s, top_i = lax.top_k(sk, PEER_TOPK)
    n_cand = PEER_TOPK * PEER_TOPK
    cand_s = (top_s[..., 0, :, None] + top_s[..., 1, None, :]).reshape(B, S, PEER_HEADS, n_cand)
    cand_i = (top_i[..., 0, :, None] * PEER_NKEYS + top_i[..., 1, None, :]).reshape(B, S, PEER_HEADS, n_cand)
    best_s, best_pos = lax.top_k(cand_s, PEER_TOPK)
    expert_idx = jnp.take_along_axis(cand_i, best_pos, axis=-1)
    gates = jax.nn.softmax(best_s, axis=-1)
    n_sel = PEER_HEADS * PEER_TOPK
    nc = (B * S) // PEER_CHUNK
    h_c = h.reshape(nc, PEER_CHUNK, D)
    idx_c = expert_idx.reshape(nc, PEER_CHUNK, n_sel)
    g_c = gates.astype(h.dtype).reshape(nc, PEER_CHUNK, n_sel)

    def chunk(args):
        hc, ic, gc = args
        act = jax.nn.gelu(jnp.einsum('tkd,td->tk', jnp.take(u, ic, axis=0), hc), approximate=False)
        return jnp.einsum('tk,tkd->td', gc * act, jnp.take(v, ic, axis=0))

    return lax.map(chunk, (h_c, idx_c, g_c)).reshape(B, S, D)

def setup_inputs(seed: int = 0) -> dict:
    key = jax.random.key(seed)
    ks = jax.random.split(key, 20)
    f32 = jnp.float32
    d = D_MODEL
    x = jax.random.normal(ks[0], (BATCH, SEQ, d), f32)
    c = jax.random.normal(ks[1], (BATCH, d), f32)
    offsets = jax.random.randint(ks[2], (BATCH, 1), 0, 512, dtype=jnp.int32)
    positions = (offsets + jnp.arange(SEQ, dtype=jnp.int32)[None, :]).astype(jnp.int32)
    ada_w = jax.random.normal(ks[3], (DEPTH, d, N_MOD * d), f32) * d ** -0.5
    ada_b = jax.random.normal(ks[4], (DEPTH, N_MOD * d), f32) * 0.02
    norm1_g = 1.0 + 0.02 * jax.random.normal(ks[5], (DEPTH, d), f32)
    w_in = jax.random.normal(ks[6], (DEPTH, d, IN_COLS), f32) * d ** -0.5
    swa_sinks = jax.random.normal(ks[7], (DEPTH, SWA_Q_HEADS), f32) * 0.5
    w_branch_swa = jax.random.normal(ks[8], (DEPTH, SWA_WIDTH, d), f32) * SWA_WIDTH ** -0.5
    w_branch_sb = jax.random.normal(ks[9], (DEPTH, SB_WIDTH, d), f32) * SB_WIDTH ** -0.5
    w_out = jax.random.normal(ks[10], (DEPTH, d, d), f32) * d ** -0.5
    norm2_g = 1.0 + 0.02 * jax.random.normal(ks[11], (DEPTH, d), f32)
    peer_wq = jax.random.normal(ks[12], (DEPTH, d, PEER_HEADS * PEER_QDIM), f32) * d ** -0.5
    peer_subkeys = jax.random.normal(ks[13], (DEPTH, PEER_HEADS, 2, PEER_NKEYS, PEER_HALF), f32) * PEER_HALF ** -0.5
    peer_u = jax.random.normal(ks[14], (DEPTH, PEER_EXPERTS, d), f32) * d ** -0.5
    peer_v = jax.random.normal(ks[15], (DEPTH, PEER_EXPERTS, d), f32) * PEER_HEADS ** -0.5
    final_g = 1.0 + 0.02 * jax.random.normal(ks[16], (d,), f32)
    return {"x": x, "c": c, "positions": positions, "ada_w": ada_w, "ada_b": ada_b,
            "norm1_g": norm1_g, "w_in": w_in, "swa_sinks": swa_sinks,
            "w_branch_swa": w_branch_swa, "w_branch_sb": w_branch_sb, "w_out": w_out,
            "norm2_g": norm2_g, "peer_wq": peer_wq, "peer_subkeys": peer_subkeys,
            "peer_u": peer_u, "peer_v": peer_v, "final_g": final_g}

def reference(x, c, positions, ada_w, ada_b, norm1_g, w_in, swa_sinks, w_branch_swa, w_branch_sb,
              w_out, norm2_g, peer_wq, peer_subkeys, peer_u, peer_v, final_g):
    B, S = x.shape[0], x.shape[1]
    c_act = jax.nn.silu(c)
    for l in range(DEPTH):
        mod = c_act @ ada_w[l] + ada_b[l]
        shift1, scale1, gate1, shift2, scale2, gate2 = [m[:, None, :] for m in jnp.split(mod, N_MOD, axis=-1)]
        h = rms_norm(x, norm1_g[l]) * (1.0 + scale1) + shift1
        proj = h @ w_in[l]
        q_a, k_a, v_a, q_b, k_b, v_b, g_a, g_b = jnp.split(proj, IN_SPLITS, axis=-1)
        q_a = apply_rope(q_a.reshape(B, S, SWA_Q_HEADS, HEAD_DIM), positions)
        k_a = apply_rope(k_a.reshape(B, S, SWA_KV_HEADS, HEAD_DIM), positions)
        y_a = sliding_window_attention(q_a, k_a, v_a.reshape(B, S, SWA_KV_HEADS, HEAD_DIM), swa_sinks[l])
        y_b = stick_breaking_attention(q_b.reshape(B, S, SB_HEADS, HEAD_DIM),
                                       k_b.reshape(B, S, SB_HEADS, HEAD_DIM),
                                       v_b.reshape(B, S, SB_HEADS, HEAD_DIM))
        merged = (jax.nn.sigmoid(g_a) * (y_a @ w_branch_swa[l])
                  + jax.nn.sigmoid(g_b) * (y_b @ w_branch_sb[l]))
        x = x + gate1 * (merged @ w_out[l])
        h2 = rms_norm(x, norm2_g[l]) * (1.0 + scale2) + shift2
        x = x + gate2 * peer_ffn(h2, peer_wq[l], peer_subkeys[l], peer_u[l], peer_v[l])
    return rms_norm(x, final_g)


_drawn_inputs = setup_inputs


def setup_inputs(seed=0):
    import zlib

    import numpy as np

    out = dict(_drawn_inputs(seed))
    spreads = {}
    factors = {'swa_sinks': 5.8, 'final_g': 2.815}
    for name, (base, spread) in spreads.items():
        noise = np.random.default_rng([zlib.crc32(name.encode()), seed]).standard_normal(out[name].shape)
        drawn = base * np.exp(spread * noise) if base else spread * noise
        out[name] = __import__('jax').numpy.asarray(drawn.astype(out[name].dtype))
    for name, factor in factors.items():
        out[name] = (out[name] * factor).astype(out[name].dtype)
    return out
```

```python
from contextlib import ExitStack

import numpy as np

import concourse.bass as bass
from concourse import mybir

F32 = mybir.dt.float32
F32R = mybir.dt.float32r
I32 = mybir.dt.int32
U32 = mybir.dt.uint32
ACT = mybir.ActivationFunctionType
ALU = mybir.AluOpType
AX = mybir.AxisListType

P = 128
D = 1024
KD = D // P
T = 256
TT = T // P
HD = 64
CH = KD * P
RAW = 4
W = 4
AHEAD = 3

N_PAR, N_ADA, N_QK, N_V, N_PAD, N_G, N_BR, N_OUT, N_WQ, N_U, N_VV = 4, 48, 13, 5, 2, 16, 8, 8, 16, 128, 128
A0 = N_PAR
M0 = A0 + N_ADA
CHUNKS = M0 + N_QK + N_V + N_PAD + N_G + N_BR + N_OUT + N_WQ + N_U + N_VV
SPLITS = CHUNKS - M0
M_QK = 0
M_V = M_QK + N_QK
M_PAD = M_V + N_V
M_G = M_PAD + N_PAD
M_BR = M_G + N_G
M_OUT = M_BR + N_BR
M_WQ = M_OUT + N_OUT
M_U = M_WQ + N_WQ
M_VV = M_U + N_U
assert CHUNKS % RAW == 0 and M0 % RAW == 0 and M_G % W == 0 and M_U % W == 0

E_QKVG = 0
E_WQ = E_QKVG + N_QK + N_V + N_G
E_SK = E_WQ + N_WQ
E_U = E_SK + 8
EVACS = E_U + N_U // 2
assert EVACS % 2 == 0

HALF = 64
GT = 8
NG = T // GT
ITERS = HALF // 4
LAST_HEAD = [5, 6, 7, 8, 10, 12, 14, 16]
UNITS = 16

C_ID, C_TRI, C_ONE, C_ROT = 0, 128, 256, 384
C_SWB = 512
C_SBM = C_SWB + 384
C_IOTA = C_SBM + 256
C_MISC = C_IOTA + 128
NCONST = C_MISC + 4

B_QK = 0
B_VT = B_QK + 13 * T
B_GT = B_VT + TT * 640
B_Y = B_GT + 16 * T
B_MG = B_Y + KD * T
B_AT = B_MG + KD * T
RU = 8
B_SQ = B_GT
B_H = B_MG
HB = HALF * T
B_QP = HB
B_SKV = B_QP + 16 * T
B_TK = B_SKV + 16 * 256
B_SUB = 2 * HB - 16 * P
B_RSTD = B_SUB - T
K_CUR, K_CUT, K_VAL, K_CAND, K_CCUT, K_REC, K_BEST8, K_POS = 0, 256, 512, 544, 800, 1056, 1120, 1136
K_BEST = 1152
K_RECS = K_BEST + 256
K_IDX = K_RECS + 16 * 64
K_PREC = K_IDX + 768
K_PEQ = K_PREC + 64
K_PRES = K_PEQ + 256
K_EXP = K_PRES + 32
K_SUM = K_EXP + 256
assert B_AT + RU * 4 * 384 <= B_RSTD and B_TK + K_SUM + 32 <= B_RSTD

NEG = -1e30
LOWEST = -3.0e38
TWO_PI_1 = 6.28125
TWO_PI_2 = float(np.float32(2 * np.pi - TWO_PI_1) // 2 ** -19 * 2 ** -19)
TWO_PI_3 = float(2 * np.pi - TWO_PI_1 - TWO_PI_2)
PI_DOWN = 3.1415925
ROUND = 12582912.0


def constants():
    c = np.zeros((P, NCONST), np.float32)
    a = np.arange(P)
    c[:, C_ID:C_ID + P] = np.eye(P)
    c[:, C_TRI:C_TRI + P] = a[:, None] >= a[None, :]
    c[:, C_ONE:C_ONE + P] = 1.0
    for d in range(P):
        lo = d % HD < HD // 2
        c[d + HD // 2 if lo else d - HD // 2, C_ROT + d] = -1.0 if lo else 1.0
    q, k = a[:, None], a[None, :]
    c[:, C_SWB:C_SWB + P] = np.where(k <= q, 0.0, NEG)
    diff = q + P - np.arange(T)[None, :]
    c[:, C_SWB + P:C_SWB + P + T] = np.where((diff >= 0) & (diff < 128), 0.0, NEG)
    c[:, C_SBM:C_SBM + T] = a[:, None] < np.arange(T)[None, :]
    c[:, C_IOTA:C_IOTA + P] = a[None, :]
    half = HD // 2
    inv = np.power(np.float32(10000.0), -np.arange(half, dtype=np.float32) * np.float32(2.0 / HD))
    c[:, C_MISC] = inv[a % half]
    c[:, C_MISC + 1] = 1e-6
    c[:, C_MISC + 2] = 1.0
    return c



def build(nc, depth, consts, stream, xT, cT, pos, final_g, outT):
    with ExitStack() as ctx:
        def sb(name, shape, dt=F32):
            return ctx.enter_context(nc.sbuf_tensor(name, shape, dt))

        def sem(name):
            return ctx.enter_context(nc.semaphore(name))

        big = sb("big", [P, 2 * HB])
        raw = sb("raw", [P, RAW, CH])
        wsp = sb("wsp", [P, W, 2, CH], F32R)
        hs = sb("hs", [P, 2, KD * T], F32R)
        x = sb("x", [P, KD * T])
        con = sb("con", [P, NCONST])
        cosT = sb("cosT", [P, T])
        sinT = sb("sinT", [P, T])
        selT = sb("selT", [P, 3, T])
        selc = sb("selc", [P, 2, 3, GT])
        ohi = sb("ohi", [P, 2, GT, P])
        ohj = sb("ohj", [P, 2, GT, HALF])
        cact = sb("cact", [P, 2 * KD])
        par = sb("par", [P, 72])
        mod = sb("mod", [P, 48])
        gs = sb("gs", [P, 2 * KD])
        fg = sb("fg", [P, KD])
        st = sb("st", [P, 4, 16])

        acc = ctx.enter_context(nc.psum_tensor("acc", [P, 2, 512], F32))
        pg = ctx.enter_context(nc.psum_tensor("pg", [P, 2, 512], F32))
        yac = ctx.enter_context(nc.psum_tensor("yac", [P, 4, 512], F32))

        inputs_in = sem("inputs_in")
        landed = [sem(f"landed{s}") for s in range(RAW)]
        params_taken = sem("params_taken")
        ada_used = sem("ada_used")
        hi_done = sem("hi_done")
        split_done = sem("split_done")
        chunk_done = sem("chunk_done")
        acc_free = sem("acc_free")
        pg_free = sem("pg_free")
        credits = sem("credits")
        cact_ready = sem("cact_ready")
        angle_done = sem("angle_done")
        rope_table = sem("rope_table")
        mod_ready = sem("mod_ready")
        sq_done = sem("sq_done")
        ssq_done = sem("ssq_done")
        std_done = sem("std_done")
        xn_done = sem("xn_done")
        src_hi = sem("src_hi")
        src_done = sem("src_done")
        rot_done = sem("rot_done")
        rope_done = sem("rope_done")
        sc_done = sem("sc_done")
        d1_done = sem("d1_done")
        a1_done = sem("a1_done")
        d2_done = sem("d2_done")
        b_done = sem("b_done")
        d3_done = sem("d3_done")
        a2_done = sem("a2_done")
        d4_done = sem("d4_done")
        av_done = sem("av_done")
        y_taken = sem("y_taken")
        sig_done = sem("sig_done")
        sk_done = sem("sk_done")
        topk_done = sem("topk_done")
        decode_done = sem("decode_done")
        gexp_in = sem("gexp_in")
        gexp_done = sem("gexp_done")
        gates_ready = sem("gates_ready")
        selT_done = sem("selT_done")
        oh_done = sem("oh_done")
        g_done = sem("g_done")
        mul_done = sem("mul_done")
        ahi_done = sem("ahi_done")
        alo_done = sem("alo_done")
        ytok_taken = sem("ytok_taken")
        yT_done = sem("yT_done")
        xT_taken = sem("xT_taken")
        out_ready = sem("out_ready")
        out_stored = sem("out_stored")
        dve_step = sem("dve_step")
        act_step = sem("act_step")
        pool_step = sem("pool_step")

        def col(base, n=1):
            return big[:, base:base + n]

        ident = con[:, C_ID:C_ID + P]
        tri = con[:, C_TRI:C_TRI + P]
        ones = con[:, C_ONE:C_ONE + P]
        rot = con[:, C_ROT:C_ROT + P]
        iota = con[:, C_IOTA:C_IOTA + P]
        iota16 = con[:, C_IOTA:C_IOTA + 16]
        invf = con[:, C_MISC:C_MISC + 1]
        eps = con[:, C_MISC + 1:C_MISC + 2]
        one = con[:, C_MISC + 2:C_MISC + 3]
        rstd = col(B_RSTD, T)
        sinks = par[:, 64:72]

        def qk(c):
            return col(B_QK + c * T, T)

        def vtok(t):
            return col(B_VT + t * 640, 640)

        def att(u, b):
            return col(B_AT + ((u % RU) * 4 + b) * 384, 384)

        def top(base, n):
            return col(B_TK + base, n)

        def half_of(h):
            return big[:, h * HB:(h + 1) * HB]

        class Steps:

            def __init__(self, eng, s):
                self.eng, self.s, self.n = eng, s, 0

            def mark(self, ins):
                self.n += 1
                ins.then_inc(self.s, 1)

            def join(self):
                self.eng.wait_ge(self.s, self.n)

            def link(self, ins):
                self.mark(ins)
                self.join()

            def clear(self):
                if self.n:
                    self.join()
                    self.eng.sem_clear(self.s)
                    self.n = 0

        def nth(L, per_layer, k, i=0, per=0):
            return L * per_layer + i * per + k

        def raw_landed(eng, L, n, i=0):
            eng.wait_ge(landed[n % RAW], nth(L, CHUNKS // RAW * 16, (n // RAW + 1) * 16, i, 16))

        def act_high(act, L, m, i=0):
            raw_landed(act, L, M0 + m, i)
            act.wait_ge(chunk_done, nth(L, SPLITS, m + 1, i, 4))
            n = P if M_PAD <= m < M_G and isinstance(i, int) else CH
            nc.scalar.activation(wsp[:, m % W, 0, 0:n], raw[:, m % RAW, 0:n],
                                 ACT.Copy).then_inc(hi_done, 1)

        def dve_low(dve, L, m, i=0):
            dve.wait_ge(hi_done, nth(L, SPLITS, m + 1, i, 4))
            n = P if M_PAD <= m < M_G and isinstance(i, int) else CH
            nc.vector.tensor_tensor(wsp[:, m % W, 1, 0:n], raw[:, m % RAW, 0:n],
                                    wsp[:, m % W, 0, 0:n].bitcast(F32),
                                    ALU.subtract).then_inc(split_done, 1)

        def chunk_split(pe, L, m, i=0):
            pe.wait_ge(split_done, nth(L, SPLITS, RAW + m + 1, i, 4))

        def chunk_used(eng, L, m, i=0):
            eng.wait_ge(chunk_done, nth(L, SPLITS, W + m + 1, i, 4))

        TERMS = ((0, 1), (1, 0), (0, 0))

        def product(pe, out, m, k0=0, k1=KD):
            mm = None
            for k in range(k0, k1):
                for n, (a, b) in enumerate(TERMS):
                    mm = pe.matmul(out, wsp[:, m % W, a, k * P:(k + 1) * P], hs[:, b, k * T:(k + 1) * T],
                                   start=(k == k0 and n == 0), stop=(k == k1 - 1 and n == 2))
            return mm

        block = ctx.enter_context(nc.Block())

        @block.sync
        def _(sp):
            sp.dma_start(con[:, :], consts).then_inc(inputs_in, 16)
            sp.dma_start(x[:, :], xT).then_inc(inputs_in, 16)
            sp.dma_start(cact[:, 0:KD], cT).then_inc(inputs_in, 16)
            sp.dma_start(cosT[:, :].bitcast(I32), pos).then_inc(inputs_in, 16)
            sp.dma_start(fg[:, :], final_g).then_inc(inputs_in, 16)

            def load(L, n, i=0, cols=CH):
                src = stream[bass.ds(nth(L, CHUNKS, n, i, 4), 1), :, 0:cols]
                sp.dma_start(raw[:, n % RAW, 0:cols],
                             src.rearrange("a p c -> p (a c)")).then_inc(landed[n % RAW], 16)

            sp.wait_ge(credits, 2)
            with sp.Fori(0, depth, 1) as L:
                for n in range(N_PAR):
                    sp.wait_ge(split_done, nth(L, SPLITS, n + 1))
                    load(L, n, cols=CH if n in (1, 2) else P)
                for n in range(N_PAR, 2 * N_PAR):
                    sp.wait_ge(params_taken, nth(L, N_PAR, n - N_PAR + 1))
                    load(L, n)
                with sp.Fori(0, N_ADA // 4, 1) as i:
                    for c in range(4):
                        sp.wait_ge(ada_used, nth(L, N_ADA, c + 1, i, 4))
                        load(L, M0 - N_ADA + N_PAR + c, i)
                with sp.Fori(0, (SPLITS - RAW) // 4, 1) as i:
                    for c in range(4):
                        sp.wait_ge(split_done, nth(L, SPLITS, RAW + c + 1, i, 4))
                        load(L, M0 + RAW + c, i)
            sp.wait_ge(out_ready, KD)
            sp.dma_start(outT, col(B_H, KD * T)).then_inc(out_stored, 16)
            sp.wait_ge(out_stored, 16)

        @block.tensor
        def _(pe):
            pe.sem_inc(chunk_done, W)

            def ssq(n, count):
                pe.wait_ge(sq_done, count)
                for k in range(KD):
                    mm = pe.matmul(yac[:, 1, 0:T], ones, col(B_SQ + k * T, T),
                                   start=(k == 0), stop=(k == KD - 1))
                mm.then_inc(ssq_done, 1)

            def by_features(L, m, e, i=0):
                chunk_split(pe, L, m, i)
                pe.wait_ge(acc_free, nth(L, EVACS, e + 1, i, 4))
                product(pe, acc[:, e % 2, 0:T], m).then_inc(chunk_done, 1)

            def by_tokens(L, m, e):
                chunk_split(pe, L, m)
                pe.wait_ge(acc_free, nth(L, EVACS, e + 1))
                for t in range(TT):
                    for k in range(KD):
                        for n, (a, b) in enumerate(TERMS):
                            mm = pe.matmul(acc[:, e % 2, t * P:(t + 1) * P],
                                           hs[:, b, k * T + t * P:k * T + (t + 1) * P],
                                           wsp[:, m % W, a, k * P:(k + 1) * P],
                                           start=(k == 0 and n == 0), stop=(k == KD - 1 and n == 2))
                mm.then_inc(chunk_done, 1)

            def rotate(L, n):
                c = n if n < 4 else 12
                e = E_QKVG + c
                pe.wait_ge(acc_free, nth(L, EVACS, e + 3))
                out = pg[:, n // 2, n % 2 * T:(n % 2 + 1) * T] if n < 4 else yac[:, 0, 0:T]
                pe.matmul(out, rot, qk(c), start=True, stop=True).then_inc(rot_done, 1)

            def head_scores(L, u):
                out = pg[:, u % 2, :]
                if u < 2:
                    pe.wait_ge(rope_done, nth(L, 5, 5))
                if u >= 2:
                    pe.wait_ge(d1_done, nth(L, UNITS, u - 1))
                if u < 8:
                    b, q, k = HD * (u // 4), qk(u % 4), qk(12)
                    pe.matmul(out[:, 0:P], q[b:b + HD, 0:P], k[b:b + HD, 0:P], start=True, stop=True)
                    mm = pe.matmul(out[:, P:384], q[b:b + HD, P:T], k[b:b + HD, 0:T], start=True, stop=True)
                else:
                    h = u - 8
                    b, q, k = HD * (h % 2), qk(4 + h // 2), qk(8 + h // 2)
                    pe.matmul(out[:, 0:T], k[b:b + HD, 0:P], q[b:b + HD, 0:T], start=True, stop=True)
                    mm = pe.matmul(out[:, T:384], k[b:b + HD, P:T], q[b:b + HD, P:T], start=True, stop=True)
                mm.then_inc(sc_done, 1)

            def head_middle(L, u):
                out = yac[:, u % 2, :]
                pe.wait_ge(d2_done, nth(L, UNITS, u + 1))
                if 2 <= u < 10:
                    pe.wait_ge(a2_done, nth(L, UNITS, u - 1))
                elif u >= 10:
                    pe.wait_ge(d3_done, nth(L, 8, u - 9))
                if u < 8:
                    for j in range(3):
                        mm = pe.transpose(out[:, j * P:(j + 1) * P], att(u, 1)[:, j * P:(j + 1) * P], ident)
                else:
                    s = att(u, 3)
                    pe.matmul(out[:, 0:T], tri, s[:, 0:T], start=True, stop=False, skip_group_check=True)
                    pe.matmul(out[:, P:T], ones, s[:, T:384], start=False, stop=True, skip_group_check=True)
                    mm = pe.matmul(out[:, T:384], tri, s[:, T:384], start=True, stop=True, skip_group_check=True)
                mm.then_inc(b_done, 1)

            def head_values(L, u):
                if u < 8:
                    pe.wait_ge(a2_done, nth(L, UNITS, u + 1))
                    b, vc = HD * (u // 4), HD * (u // 4)
                else:
                    h = u - 8
                    pe.wait_ge(d4_done, nth(L, 8, h + 1))
                    b, vc = HD * (h % 2), P + HD * h
                w = att(u, 2)
                if u >= 2:
                    pe.wait_ge(y_taken, nth(L, UNITS, u - 1))
                out = yac[b:b + HD, 2 + u % 2, :]
                pe.matmul(out[:, 0:T], vtok(0)[:, vc:vc + HD], w[:, 0:T], start=True, stop=False,
                          skip_group_check=True)
                pe.matmul(out[:, P:T], vtok(1)[:, vc:vc + HD], w[:, T:384], start=False, stop=True,
                          skip_group_check=True).then_inc(av_done, 1)

            def expert_pair(L, half, c, i):
                m = M_U + half * HALF + c
                e = E_U + (half * HALF + c) // 2
                pe.wait_ge(acc_free, nth(L, EVACS, e + 1, i, 2))
                for a in range(2):
                    chunk_split(pe, L, m + a, i)
                    product(pe, acc[:, e % 2, a * T:(a + 1) * T], m + a).then_inc(chunk_done, 1)

            def gate_group(L, half, g, i):
                k = half * NG + g
                pe.wait_ge(oh_done, nth(L, 2 * NG, k + 1, i, 2))
                pe.wait_ge(mul_done, nth(L, 2 * NG, k + 1, i, 2))
                for t in range(GT):
                    mm = pe.matmul(pg[:, g, t * HALF:(t + 1) * HALF], ohi[:, g, t, :], ohj[:, g, t, :],
                                   start=True, stop=True)
                mm.then_inc(g_done, 1)

            def value_chunk(L, half, c, i, start=False, stop=False):
                m = M_VV + half * HALF + c
                if c % 2 == 0:
                    pe.wait_ge(alo_done, nth(L, HALF, (half * HALF + c) // 2 + 1, i, 2))
                chunk_split(pe, L, m, i)
                for t in range(TT):
                    for n, (a, b) in enumerate(TERMS):
                        for w in range(2):
                            mm = pe.matmul(yac[:, 2 * t + w, :], hs[:, b, c * T + t * P:c * T + (t + 1) * P],
                                           wsp[:, m % W, a, w * 512:(w + 1) * 512],
                                           start=(start and n == 0), stop=(stop and n == 2),
                                           skip_group_check=True)
                mm.then_inc(chunk_done, 1)

            pe.wait_ge(inputs_in, 80)
            pe.wait_ge(cact_ready, 1)
            with pe.Fori(0, depth, 1) as L:
                with pe.Fori(0, N_ADA // 4, 1) as i:
                    for c in range(4):
                        raw_landed(pe, L, N_PAR + c, i)
                        for k in range(KD):
                            mm = pe.matmul(yac[:, 0, bass.ds(i * 4 + c, 1)],
                                           raw[:, c, k * P:(k + 1) * P], cact[:, KD + k:KD + k + 1],
                                           start=(k == 0), stop=(k == KD - 1), skip_group_check=True)
                        mm.then_inc(ada_used, 1)
                ssq(0, nth(L, 2, 1))
                with pe.Fori(0, 3, 1) as i:
                    pe.wait_ge(src_done, nth(L, 4 * KD, KD))
                    for c in range(4):
                        by_features(L, M_QK + c, E_QKVG + c, i)
                by_features(L, M_QK + 12, E_QKVG + 12)
                for c in range(N_V):
                    by_tokens(L, M_V + c, E_QKVG + N_QK + c)
                for m in range(M_PAD, M_G):
                    chunk_split(pe, L, m)
                    pe.matmul(yac[:, 2, 0:2], wsp[:, m % W, 0, 0:P], wsp[:, m % W, 1, 0:2],
                              start=True, stop=True).then_inc(chunk_done, 1)
                for n in range(5):
                    rotate(L, n)
                for s in range(UNITS + 5):
                    if s < N_G:
                        by_features(L, M_G + s, E_QKVG + N_QK + N_V + s)
                    if s < UNITS:
                        head_scores(L, s)
                    if 2 <= s < UNITS + 2:
                        head_middle(L, s - 2)
                    if 4 <= s < UNITS + 4:
                        head_values(L, s - 4)
                with pe.Fori(0, N_BR // 4, 1) as i:
                    pe.wait_ge(src_done, nth(L, 4 * KD, 2 * KD))
                    for c in range(4):
                        chunk_split(pe, L, M_BR + c, i)
                        pe.wait_ge(pg_free, nth(L, N_BR + N_OUT, c + 1, i, 4))
                        product(pe, pg[:, c % 2, 0:T], M_BR + c, 0, 4)
                        product(pe, pg[:, c % 2, T:2 * T], M_BR + c, 4, 8).then_inc(chunk_done, 1)
                with pe.Fori(0, N_OUT // 4, 1) as i:
                    pe.wait_ge(src_done, nth(L, 4 * KD, 3 * KD))
                    for c in range(4):
                        chunk_split(pe, L, M_OUT + c, i)
                        pe.wait_ge(pg_free, nth(L, N_BR + N_OUT, N_BR + c + 1, i, 4))
                        product(pe, pg[:, c % 2, 0:T], M_OUT + c).then_inc(chunk_done, 1)
                ssq(1, nth(L, 2, 2))
                with pe.Fori(0, N_WQ // 4, 1) as i:
                    pe.wait_ge(src_done, nth(L, 4 * KD, 4 * KD))
                    for c in range(4):
                        by_features(L, M_WQ + c, E_WQ + c, i)
                for e in range(8):
                    t, q = e // 4, e % 4
                    pe.wait_ge(acc_free, nth(L, EVACS, E_SK + e + 1 if e > 1 else E_SK + 2))
                    for n in range(4):
                        mm = pe.matmul(acc[:, e % 2, n * P:(n + 1) * P],
                                       col(B_QP + (4 * q + n) * T + t * P, P),
                                       col(B_SUB + (4 * q + n) * P, P), start=True, stop=True)
                    mm.then_inc(sk_done, 1)
                with pe.Fori(0, ITERS, 1) as i:
                    for c in (0, 2):
                        expert_pair(L, 0, c, i)
                pe.wait_ge(gates_ready, nth(L, 1, 1))
                for t in range(TT):
                    for n in range(3):
                        mm = pe.transpose(pg[:, t, n * P:(n + 1) * P], top(K_IDX + n * T + t * P, P), ident)
                mm.then_inc(selT_done, 1)
                with pe.Fori(0, ITERS, 1) as i:
                    for g in range(2):
                        expert_pair(L, 1, 2 * g, i)
                        gate_group(L, 0, g, i)

                def values_and_gates(i, start=False):
                    for g in range(2):
                        value_chunk(L, 0, 2 * g, i, start=start and g == 0)
                        value_chunk(L, 0, 2 * g + 1, i)
                        gate_group(L, 1, g, i)

                values_and_gates(0, start=True)
                with pe.Fori(1, ITERS, 1) as i:
                    values_and_gates(i)
                with pe.Fori(0, ITERS - 1, 1) as i:
                    for c in range(4):
                        value_chunk(L, 1, c, i)
                for c in range(4):
                    value_chunk(L, 1, c, ITERS - 1, stop=(c == 3))
                pe.wait_ge(ytok_taken, nth(L, 1, 1))
                for g in range(4):
                    out = acc[:, g, :] if g < 2 else pg[:, g - 2, :]
                    for k in range(2):
                        for t in range(TT):
                            mm = pe.transpose(out[:, k * T + t * P:k * T + (t + 1) * P],
                                              col(t * D + (2 * g + k) * P, P), ident)
                    mm.then_inc(yT_done, 1)
            ssq(2, 2 * depth + 1)

        @block.scalar
        def _(act):
            a = Steps(act, act_step)
            act.sem_inc(acc_free, 2)
            nc_act = nc.scalar

            def rms(count):
                nc_act.activation(col(B_SQ, KD * T), x[:, :], ACT.Square).then_inc(sq_done, 1)
                act.wait_ge(ssq_done, count)
                nc_act.activation(rstd, yac[:, 1, 0:T], ACT.Sqrt, bias=eps,
                                  scale=1.0 / D).then_inc(std_done, 1)

            def modulated(L, w):
                for k in range(KD):
                    act.wait_ge(xn_done, nth(L, 2 * KD, w * KD + k + 1))
                    h = col(B_H + k * T, T)
                    a.link(nc_act.activation(h, h, ACT.Identity, bias=mod[:, 24 * w + k:24 * w + k + 1],
                                             scale=gs[:, KD * w + k:KD * w + k + 1]))
                    nc_act.activation(hs[:, 0, k * T:(k + 1) * T], h, ACT.Copy).then_inc(src_hi, 1)

            def store(L, m, e, dst, i=0):
                chunk_used(act, L, m, i)
                nc_act.activation(dst, acc[:, e % 2, 0:T], ACT.Copy).then_inc(acc_free, 1)

            def head_a1(L, u):
                act.wait_ge(d1_done, nth(L, UNITS, u + 1))
                s = st[:, u % 4, :]
                if u < 8:
                    for b in range(2):
                        lo, hi = (0, P) if b == 0 else (P, 384)
                        nc_act.activation(att(u, 1)[:, lo:hi], att(u, 0)[:, lo:hi], ACT.Exp,
                                          bias=s[:, 2 + b:3 + b], accum_out=s[:, 4 + b:5 + b])
                    nc_act.activation(s[:, 6:8], s[:, 2:4], ACT.Exp,
                                      bias=sinks[:, u:u + 1]).then_inc(a1_done, 1)
                else:
                    a.link(nc_act.activation(att(u, 1), att(u, 0), ACT.Abs))
                    a.link(nc_act.activation(att(u, 2), att(u, 1), ACT.Exp, scale=-1.0))
                    nc_act.activation(att(u, 1), att(u, 2), ACT.Ln, bias=one).then_inc(a1_done, 1)

            def head_a2(L, u):
                if u < 8:
                    act.wait_ge(b_done, nth(L, UNITS, u + 1))
                    nc_act.activation(att(u, 2), yac[:, u % 2, 0:384], ACT.Copy).then_inc(a2_done, 1)
                else:
                    act.wait_ge(d3_done, nth(L, 8, u - 8 + 1))
                    nc_act.activation(att(u, 1), att(u, 3), ACT.Exp).then_inc(a2_done, 1)

            def gelu_pair(L, half, c, i):
                m = M_U + half * HALF + c
                e = E_U + (half * HALF + c) // 2
                chunk_used(act, L, m + 1, i)
                nc_act.activation(half_of(half)[:, bass.ds(nth(i, 4 * T, c * T), 2 * T)],
                                  acc[:, e % 2, :], ACT.Gelu).then_inc(acc_free, 1)

            def a_high(L, half, q, i):
                r = half * (HALF // 2) + q
                if q > 1 or not isinstance(i, int) or i:
                    chunk_used(act, L, M_VV + 2 * r - 3, i)
                nc_act.activation(hs[:, 0, q % 2 * 2 * T:(q % 2 + 1) * 2 * T],
                                  half_of(half)[:, bass.ds(nth(i, 4 * T, 2 * q * T), 2 * T)],
                                  ACT.Copy).then_inc(ahi_done, 1)

            act.wait_ge(inputs_in, 80)
            nc_act.activation(cact[:, KD:2 * KD], cact[:, 0:KD], ACT.Silu).then_inc(cact_ready, 1)
            act.wait_ge(angle_done, 1)
            nc_act.activation(sinT[:, :], col(B_AT, T), ACT.Sin)
            nc_act.activation(cosT[:, :], col(B_AT + T, T), ACT.Sin).then_inc(rope_table, 1)
            with act.Fori(0, depth, 1) as L:
                act.wait_ge(xT_taken, nth(L, 4, 4))
                rms(nth(L, 2, 1))
                for m in range(AHEAD):
                    act_high(act, L, m)
                act.wait_ge(mod_ready, nth(L, 1, 1))
                modulated(L, 0)
                a.clear()
                with act.Fori(0, 3, 1) as i:
                    for c in range(4):
                        act_high(act, L, M_QK + c + AHEAD, i)
                        store(L, M_QK + c, E_QKVG + c, big[:, bass.ds(nth(i, 4 * T, B_QK + c * T), T)], i)
                act_high(act, L, M_QK + 12 + AHEAD)
                store(L, M_QK + 12, E_QKVG + 12, qk(12))
                for c in range(N_V):
                    e = E_QKVG + N_QK + c
                    act_high(act, L, M_V + c + AHEAD)
                    chunk_used(act, L, M_V + c)
                    dst = col(B_VT, TT * 640).rearrange("p (t f) -> p t f", t=TT)[:, :, c * P:(c + 1) * P]
                    nc_act.activation(dst, acc[:, e % 2, 0:T].rearrange("p (t f) -> p t f", t=TT),
                                      ACT.Copy).then_inc(acc_free, 1)
                for m in range(M_PAD, M_G):
                    act_high(act, L, m + AHEAD)
                for s in range(UNITS + 5):
                    if s < N_G:
                        act_high(act, L, M_G + s + AHEAD)
                    if 1 <= s <= N_G:
                        store(L, M_G + s - 1, E_QKVG + N_QK + N_V + s - 1, col(B_GT + (s - 1) * T, T))
                    if 1 <= s < UNITS + 1:
                        head_a1(L, s - 1)
                    if 3 <= s < UNITS + 3:
                        head_a2(L, s - 3)
                for k in range(KD):
                    if k == 0:
                        chunk_used(act, L, M_G + N_G - 1)
                    act.wait_ge(y_taken, nth(L, UNITS, LAST_HEAD[k]))
                    nc_act.activation(hs[:, 0, k * T:(k + 1) * T], col(B_Y + k * T, T),
                                      ACT.Copy).then_inc(src_hi, 1)
                act.wait_ge(acc_free, nth(L, EVACS, E_WQ + 2))
                nc_act.activation(col(B_GT, 16 * T), col(B_GT, 16 * T), ACT.Sigmoid).then_inc(sig_done, 1)
                a.clear()
                with act.Fori(0, N_BR // 4, 1) as i:
                    for c in range(4):
                        act_high(act, L, M_BR + c + AHEAD, i)
                chunk_used(act, L, M_BR + N_BR - 1)
                for k in range(KD):
                    act.wait_ge(pg_free, nth(L, N_BR + N_OUT, 2 + k + 1))
                    nc_act.activation(hs[:, 0, k * T:(k + 1) * T], col(B_MG + k * T, T),
                                      ACT.Copy).then_inc(src_hi, 1)
                with act.Fori(0, N_OUT // 4, 1) as i:
                    for c in range(4):
                        act_high(act, L, M_OUT + c + AHEAD, i)
                act.wait_ge(pg_free, nth(L, N_BR + N_OUT, 2 + N_BR + N_OUT))
                rms(nth(L, 2, 2))
                modulated(L, 1)
                a.clear()
                with act.Fori(0, N_WQ // 4, 1) as i:
                    for c in range(4):
                        act_high(act, L, M_WQ + c + AHEAD, i)
                        store(L, M_WQ + c, E_WQ + c, big[:, bass.ds(nth(i, 4 * T, B_QP + c * T), T)], i)
                for e in range(8):
                    act.wait_ge(sk_done, nth(L, 8, e + 1))
                    nc_act.activation(col(B_SKV + e * 512, 512), acc[:, e % 2, :],
                                      ACT.Copy).then_inc(acc_free, 1)
                with act.Fori(0, ITERS, 1) as i:
                    for c in (0, 2):
                        act_high(act, L, M_U + c + AHEAD, i)
                        act_high(act, L, M_U + c + 1 + AHEAD, i)
                        gelu_pair(L, 0, c, i)
                act.wait_ge(gexp_in, nth(L, 1, 1))
                nc_act.activation(top(K_EXP, 256), top(K_EXP, 256), ACT.Exp).then_inc(gexp_done, 1)
                act.wait_ge(selT_done, nth(L, 1, 1))
                with act.Fori(0, ITERS, 1) as i:
                    for c in (0, 2):
                        act_high(act, L, M_U + HALF + c + AHEAD, i)
                        act_high(act, L, M_U + HALF + c + 1 + AHEAD, i)
                        gelu_pair(L, 1, c, i)

                def values(half, i, last=False, end=False):
                    for q in range(2):
                        if not (last and q == 1):
                            a_high(L, half, q + 1, i)
                        for c in (2 * q, 2 * q + 1):
                            if not (end and c + AHEAD >= 4):
                                act_high(act, L, M_VV + half * HALF + c + AHEAD, i)

                act.wait_ge(mul_done, nth(L, 2 * NG, 2 + NG))
                a_high(L, 0, 0, 0)
                with act.Fori(0, ITERS - 1, 1) as i:
                    values(0, i)
                values(0, ITERS - 1, last=True)
                act.wait_ge(mul_done, nth(L, 2 * NG, 2 + 2 * NG))
                chunk_used(act, L, M_VV + HALF - 3)
                a_high(L, 1, 0, 0)
                with act.Fori(0, ITERS - 1, 1) as i:
                    values(1, i)
                values(1, ITERS - 1, last=True, end=True)
                a.clear()
            act.wait_ge(xT_taken, 4 * depth + 4)
            rms(2 * depth + 1)
            for k in range(KD):
                act.wait_ge(xn_done, 2 * KD * depth + k + 1)
                h = col(B_H + k * T, T)
                nc_act.activation(h, h, ACT.Copy, scale=fg[:, k:k + 1]).then_inc(out_ready, 1)

        @block.vector
        def _(dve):
            v = nc.vector
            d = Steps(dve, dve_step)
            dve.sem_inc(split_done, RAW)
            dve.sem_inc(pg_free, 2)
            dve.sem_inc(mul_done, 2)
            dve.sem_inc(xT_taken, 4)
            dve.sem_inc(credits, 2)

            def normalised(n, count):
                dve.wait_ge(std_done, count)
                d.link(v.reciprocal(rstd, rstd))
                for k in range(KD):
                    v.tensor_tensor(col(B_H + k * T, T), x[:, k * T:(k + 1) * T], rstd,
                                    ALU.mult).then_inc(xn_done, 1)

            def source_low(L, s, src):
                for k in range(KD):
                    dve.wait_ge(src_hi, nth(L, 4 * KD, s * KD + k + 1))
                    v.tensor_tensor(hs[:, 1, k * T:(k + 1) * T], col(src + k * T, T),
                                    hs[:, 0, k * T:(k + 1) * T].bitcast(F32),
                                    ALU.subtract).then_inc(src_done, 1)

            def rope(L, n):
                c = n if n < 4 else 12
                dve.wait_ge(rot_done, nth(L, 5, n // 2 * 2 + 2 if n < 4 else 5))
                r = pg[:, n // 2, n % 2 * T:(n % 2 + 1) * T] if n < 4 else yac[:, 0, 0:T]
                d.mark(v.tensor_tensor(att(n, 0)[:, 0:T], r, sinT[:, :], ALU.mult))
                d.link(v.tensor_tensor(qk(c), qk(c), cosT[:, :], ALU.mult))
                v.tensor_tensor(qk(c), qk(c), att(n, 0)[:, 0:T], ALU.add).then_inc(rope_done, 1)

            def head_d1(L, u):
                dve.wait_ge(sc_done, nth(L, UNITS, u + 1))
                z, s = pg[:, u % 2, 0:384], st[:, u % 4, :]
                if u < 8:
                    d.link(v.scalar_tensor_tensor(att(u, 0), z, HD ** -0.5, con[:, C_SWB:C_SWB + 384],
                                                  ALU.mult, ALU.add))
                    d.mark(v.tensor_reduce(s[:, 0:1], att(u, 0)[:, 0:P], AX.X, ALU.max))
                    d.link(v.tensor_reduce(s[:, 1:2], att(u, 0)[:, P:384], AX.X, ALU.max))
                    v.tensor_scalar(s[:, 2:4], s[:, 0:2], sinks[:, u:u + 1], -1.0, ALU.max,
                                    ALU.mult).then_inc(d1_done, 1)
                else:
                    v.scalar_tensor_tensor(att(u, 0)[:, 0:T], z[:, 0:T], HD ** -0.5,
                                           con[:, C_SBM:C_SBM + T], ALU.mult, ALU.mult)
                    v.scalar_tensor_tensor(att(u, 0)[:, T:384], z[:, T:384], HD ** -0.5,
                                           con[:, C_SBM:C_SBM + P], ALU.mult, ALU.mult).then_inc(d1_done, 1)

            def masked(dst, src):
                v.tensor_tensor(dst[:, 0:T], src[:, 0:T], con[:, C_SBM:C_SBM + T], ALU.mult)
                return v.tensor_tensor(dst[:, T:384], src[:, T:384], con[:, C_SBM:C_SBM + P], ALU.mult)

            def head_d2(L, u):
                dve.wait_ge(a1_done, nth(L, UNITS, u + 1))
                s = st[:, u % 4, :]
                if u < 8:
                    d.link(v.tensor_tensor(s[:, 8:10], s[:, 4:6], s[:, 6:8], ALU.add))
                    d.link(v.reciprocal(s[:, 10:12], s[:, 8:10]))
                    p = att(u, 1)
                    v.tensor_scalar(p[:, 0:P], p[:, 0:P], s[:, 10:11], None, ALU.mult)
                    v.tensor_scalar(p[:, P:384], p[:, P:384], s[:, 11:12], None,
                                    ALU.mult).then_inc(d2_done, 1)
                else:
                    d.link(v.scalar_tensor_tensor(att(u, 2), att(u, 0), 0.0, att(u, 1), ALU.max, ALU.add))
                    masked(att(u, 3), att(u, 2)).then_inc(d2_done, 1)

            def head_d3(L, u):
                dve.wait_ge(b_done, nth(L, UNITS, u + 1))
                v.tensor_tensor(att(u, 3), att(u, 0), yac[:, u % 2, 0:384], ALU.subtract).then_inc(d3_done, 1)

            def head_d4(L, u):
                dve.wait_ge(a2_done, nth(L, UNITS, u + 1))
                masked(att(u, 2), att(u, 1)).then_inc(d4_done, 1)

            def head_out(L, u):
                dve.wait_ge(av_done, nth(L, UNITS, u + 1))
                h = u - 8
                b, c = (HD * (u // 4), u % 4) if u < 8 else (HD * (h % 2), 4 + h // 2)
                v.tensor_copy(col(B_Y + c * T, T)[b:b + HD, :],
                              yac[b:b + HD, 2 + u % 2, 0:T]).then_inc(y_taken, 1)

            def top16(values, cut, best, index):
                d.link(v.max(best[:, 0:8], values))
                d.mark(v.max_index(index[:, 0:8], best[:, 0:8], values))
                d.link(v.match_replace(cut, best[:, 0:8], values, LOWEST))
                d.link(v.max(best[:, 8:16], cut))
                d.link(v.max_index(index[:, 8:16], best[:, 8:16], cut))

            def subkey_topk(L, i):
                d.link(v.tensor_copy(top(K_CUR, 256), big[:, bass.ds(nth(i, 256, B_SKV), 256)]))
                for p in range(2):
                    top16(top(K_CUR + p * P, P), top(K_CUT, P), top(K_VAL + 16 * p, 16),
                          top(K_REC + 16 * p, 16).bitcast(U32))

            def pair_topk(L, i):
                cand = top(K_CAND, 256)
                shape = [P, 16, 16]
                d.link(v.tensor_tensor(cand.rearrange("p (a b) -> p a b", a=16),
                                       top(K_VAL, 16).unsqueeze(2).to_broadcast(shape),
                                       top(K_VAL + 16, 16).unsqueeze(1).to_broadcast(shape), ALU.add))
                pos_ = top(K_POS, 16).bitcast(U32)
                top16(cand, top(K_CCUT, 256), top(K_BEST8, 16), pos_)
                d.mark(v.tensor_copy(big[:, bass.ds(nth(i, 16, B_TK + K_BEST), 16)], top(K_BEST8, 16)))
                d.mark(v.tensor_scalar(top(K_REC + 32, 16).bitcast(U32), pos_, 4, None, ALU.logical_shift_right))
                d.link(v.tensor_scalar(top(K_REC + 48, 16).bitcast(U32), pos_, 15, None, ALU.bitwise_and))
                v.tensor_copy(big[:, bass.ds(nth(i, 64, B_TK + K_RECS), 64)],
                              top(K_REC, 64).bitcast(U32)).then_inc(topk_done, 1)

            def onehots(L, half, g, i):
                d.link(v.tensor_copy(selc[:, g, :, :], selT[:, :, bass.ds(nth(i, 2 * GT, g * GT), GT)]))
                lo = half * HALF
                for t in range(GT):
                    v.tensor_scalar(ohi[:, g, t, :], iota, selc[:, g, 0, t:t + 1], None, ALU.is_equal)
                    ins = v.tensor_scalar(ohj[:, g, t, :], iota[:, lo:lo + HALF], selc[:, g, 1, t:t + 1],
                                          selc[:, g, 2, t:t + 1], ALU.is_equal, ALU.mult)
                ins.then_inc(oh_done, 1)

            def gate(L, half, g, i, back=0):
                k = half * NG + g - back
                dve.wait_ge(g_done, nth(L, 2 * NG, k + 1, i, 2))
                dst = half_of(half).rearrange("p (j t) -> p j t", t=T)[
                    :, :, bass.ds(nth(i, 2 * GT, (g - back) * GT), GT)]
                v.tensor_tensor(dst, dst, pg[:, g, :].rearrange("p (t j) -> p j t", t=GT),
                                ALU.mult).then_inc(mul_done, 1)

            def a_low(L, half, q, i):
                dve.wait_ge(ahi_done, nth(L, HALF, half * HALF // 2 + q + 1, i, 2))
                s = slice(q % 2 * 2 * T, (q % 2 + 1) * 2 * T)
                v.tensor_tensor(hs[:, 1, s], half_of(half)[:, bass.ds(nth(i, 4 * T, 2 * q * T), 2 * T)],
                                hs[:, 0, s].bitcast(F32), ALU.subtract).then_inc(alo_done, 1)

            dve.wait_ge(inputs_in, 80)
            ang, cang, turns = col(B_AT, T), col(B_AT + T, T), col(B_AT + 2 * T, T)
            d.link(v.tensor_copy(cang, cosT[:, :].bitcast(I32)))
            d.link(v.tensor_scalar(ang, cang, invf, None, ALU.mult))
            d.link(v.tensor_scalar(turns, ang, 1.0 / (2 * np.pi), None, ALU.mult))
            d.link(v.tensor_scalar(turns, turns, ROUND, None, ALU.add))
            d.link(v.tensor_scalar(turns, turns, ROUND, None, ALU.subtract))
            for part in (TWO_PI_1, TWO_PI_2, TWO_PI_3):
                d.link(v.scalar_tensor_tensor(ang, turns, -part, ang, ALU.mult, ALU.add))
            d.link(v.tensor_scalar(cang, ang, np.pi / 2, None, ALU.add))
            d.link(v.tensor_scalar(turns, cang, np.pi, -2 * np.pi, ALU.is_gt, ALU.mult))
            d.link(v.tensor_tensor(cang, cang, turns, ALU.add))
            v.tensor_scalar(cang, cang, PI_DOWN, -PI_DOWN, ALU.min, ALU.max)
            v.tensor_scalar(ang, ang, PI_DOWN, -PI_DOWN, ALU.min, ALU.max).then_inc(angle_done, 1)
            dve.wait_ge(rope_table, 1)
            d.clear()
            with dve.Fori(0, depth, 1) as L:
                for n in range(N_PAR):
                    raw_landed(dve, L, n)
                    if n in (1, 2):
                        ins = v.tensor_copy(col(B_SUB + (n - 1) * CH, CH), raw[:, n, :])
                    else:
                        ins = v.tensor_copy(par[:, :], raw[:, n, 0:72]) if n == 0 else \
                            v.tensor_copy(st[:, 3, 15:16], raw[:, n, 0:1])
                    ins.then_inc(params_taken, 1)
                normalised(0, nth(L, 2, 1))
                dve.wait_ge(ada_used, nth(L, N_ADA, N_ADA))
                d.link(v.tensor_tensor(mod[:, :], yac[:, 0, 0:48], par[:, 0:48], ALU.add))
                d.mark(v.scalar_tensor_tensor(gs[:, 0:KD], mod[:, 8:16], 1.0, par[:, 48:56], ALU.add, ALU.mult))
                d.join()
                v.scalar_tensor_tensor(gs[:, KD:2 * KD], mod[:, 32:40], 1.0, par[:, 56:64],
                                       ALU.add, ALU.mult).then_inc(mod_ready, 1)
                for m in range(AHEAD):
                    dve_low(dve, L, m)
                source_low(L, 0, B_H)
                d.clear()
                with dve.Fori(0, 3, 1) as i:
                    for c in range(4):
                        dve_low(dve, L, c + AHEAD, i)
                for m in range(12, M_G):
                    dve_low(dve, L, m + AHEAD)
                for n in range(5):
                    rope(L, n)
                for s in range(UNITS + 5):
                    if s < N_G:
                        dve_low(dve, L, M_G + s + AHEAD)
                    if 1 <= s < UNITS + 1:
                        head_d1(L, s - 1)
                    if 2 <= s < UNITS + 2:
                        head_d2(L, s - 2)
                    if 11 <= s < UNITS + 3:
                        head_d3(L, s - 3)
                    if 12 <= s < UNITS + 4:
                        head_d4(L, s - 4)
                    if 5 <= s:
                        head_out(L, s - 5)
                source_low(L, 1, B_Y)
                d.clear()
                with dve.Fori(0, N_BR // 4, 1) as i:
                    dve.wait_ge(sig_done, nth(L, 1, 1))
                    for c in range(4):
                        dve_low(dve, L, M_BR + c + AHEAD, i)
                        chunk_used(dve, L, M_BR + c, i)
                        ga = big[:, bass.ds(nth(i, 4 * T, B_GT + c * T), T)]
                        gb = big[:, bass.ds(nth(i, 4 * T, B_GT + (8 + c) * T), T)]
                        d.mark(v.tensor_tensor(ga, ga, pg[:, c % 2, 0:T], ALU.mult))
                        d.link(v.tensor_tensor(gb, gb, pg[:, c % 2, T:2 * T], ALU.mult))
                        v.tensor_tensor(big[:, bass.ds(nth(i, 4 * T, B_MG + c * T), T)], ga, gb,
                                        ALU.add).then_inc(pg_free, 1)
                    d.clear()
                source_low(L, 2, B_MG)
                with dve.Fori(0, N_OUT // 4, 1) as i:
                    for c in range(4):
                        dve_low(dve, L, M_OUT + c + AHEAD, i)
                        chunk_used(dve, L, M_OUT + c, i)
                        xc = x[:, bass.ds(nth(i, 4 * T, c * T), T)]
                        v.scalar_tensor_tensor(xc, pg[:, c % 2, 0:T], mod[:, bass.ds(nth(i, 4, 16 + c), 1)],
                                               xc, ALU.mult, ALU.add).then_inc(pg_free, 1)
                normalised(1, nth(L, 2, 2))
                source_low(L, 3, B_H)
                with dve.Fori(0, N_WQ // 4, 1) as i:
                    for c in range(4):
                        dve_low(dve, L, M_WQ + c + AHEAD, i)
                d.clear()
                with dve.Fori(0, ITERS, 1) as i:
                    dve.wait_ge(acc_free, nth(L, EVACS, E_U + 2))
                    for c in range(4):
                        dve_low(dve, L, M_U + c + AHEAD, i)
                        if c == 1:
                            subkey_topk(L, i)
                        if c == 3:
                            pair_topk(L, i)
                    d.clear()
                best = top(K_BEST, 256).rearrange("p (u r) -> p u r", r=16)
                e3 = top(K_EXP, 256).rearrange("p (u r) -> p u r", r=16)
                v.tensor_tensor(e3, best, best[:, :, 0:1].to_broadcast([P, 16, 16]),
                                ALU.subtract).then_inc(gexp_in, 1)
                dve.wait_ge(gexp_done, nth(L, 1, 1))
                d.link(v.tensor_reduce(top(K_SUM, 16), e3, AX.X, ALU.add))
                d.link(v.reciprocal(top(K_SUM + 16, 16), top(K_SUM, 16)))
                dve.wait_ge(decode_done, nth(L, UNITS, UNITS))
                v.tensor_tensor(top(K_IDX + 512, 256).rearrange("p (u r) -> p u r", r=16), e3,
                                top(K_SUM + 16, 16).unsqueeze(2).to_broadcast([P, 16, 16]),
                                ALU.mult).then_inc(gates_ready, 1)
                dve.wait_ge(selT_done, nth(L, 1, 1))
                for t in range(TT):
                    d.mark(v.tensor_copy(selT[:, :, t * P:(t + 1) * P],
                                         pg[:, t, 0:384].rearrange("p (n t) -> p n t", n=3)))
                d.clear()

                def experts_and_gates(i, first=False):
                    for g in range(2):
                        for c in (2 * g, 2 * g + 1):
                            dve_low(dve, L, M_U + HALF + c + AHEAD, i)
                        onehots(L, 0, g, i)
                        if not (first and g == 0):
                            gate(L, 0, 1 - g, i, back=2 if g == 0 else 0)

                experts_and_gates(0, first=True)
                d.clear()
                with dve.Fori(1, ITERS, 1) as i:
                    experts_and_gates(i)
                    d.clear()
                gate(L, 0, 1, ITERS - 1)

                def values_and_gates(i, first=False, last=False):
                    for g in range(2):
                        if not (last and g == 1):
                            a_low(L, 0, g + 1, i)
                        for c in (2 * g, 2 * g + 1):
                            dve_low(dve, L, M_VV + c + AHEAD, i)
                        onehots(L, 1, g, i)
                        if not (first and g == 0):
                            gate(L, 1, 1 - g, i, back=2 if g == 0 else 0)

                a_low(L, 0, 0, 0)
                values_and_gates(0, first=True)
                d.clear()
                with dve.Fori(1, ITERS - 1, 1) as i:
                    values_and_gates(i)
                    d.clear()
                values_and_gates(ITERS - 1, last=True)
                gate(L, 1, 1, ITERS - 1)
                a_low(L, 1, 0, 0)
                with dve.Fori(0, ITERS - 1, 1) as i:
                    for q in range(2):
                        a_low(L, 1, q + 1, i)
                        for c in (2 * q, 2 * q + 1):
                            dve_low(dve, L, M_VV + HALF + c + AHEAD, i)
                a_low(L, 1, 1, ITERS - 1)
                dve_low(dve, L, M_VV + HALF + AHEAD, ITERS - 1)
                chunk_used(dve, L, SPLITS - 1)
                for t in range(TT):
                    ins = v.tensor_copy(col(t * D, D), yac[:, 2 * t:2 * t + 2, :])
                ins.then_inc(ytok_taken, 1)
                for g in range(4):
                    out = acc[:, g, :] if g < 2 else pg[:, g - 2, :]
                    dve.wait_ge(yT_done, nth(L, 4, g + 1))
                    for k in (2 * g, 2 * g + 1):
                        xc = x[:, k * T:(k + 1) * T]
                        ins = v.scalar_tensor_tensor(xc, out[:, k % 2 * T:(k % 2 + 1) * T],
                                                     mod[:, 40 + k:41 + k], xc, ALU.mult, ALU.add)
                    ins.then_inc(xT_taken, 1)
                d.clear()
            normalised(2, 2 * depth + 1)

        @block.gpsimd
        def _(pool):
            g = nc.gpsimd
            s = Steps(pool, pool_step)
            with pool.Fori(0, depth, 1) as L:
                with pool.Fori(0, UNITS, 1) as i:
                    pool.wait_ge(topk_done, nth(L, UNITS, 1, i, 1))
                    rec = top(K_PREC, 64)
                    s.link(g.tensor_copy(rec, big[:, bass.ds(nth(i, 64, B_TK + K_RECS), 64)]))
                    eq = top(K_PEQ, 256).rearrange("p (r a) -> p r a", a=16)
                    shape = [P, 16, 16]
                    for p in range(2):
                        s.link(g.tensor_tensor(eq, rec[:, 32 + 16 * p:48 + 16 * p].unsqueeze(2).to_broadcast(shape),
                                               iota16.unsqueeze(1).to_broadcast(shape), ALU.subtract))
                        s.link(g.tensor_scalar(eq, eq, 0.0, None, ALU.is_equal))
                        s.link(g.tensor_tensor(eq, eq, rec[:, 16 * p:16 * p + 16].unsqueeze(1).to_broadcast(shape),
                                               ALU.mult))
                        for n in (8, 4, 2):
                            s.link(g.tensor_tensor(eq[:, :, 0:n], eq[:, :, 0:n], eq[:, :, n:2 * n], ALU.add))
                        s.link(g.tensor_tensor(top(K_PRES + 16 * p, 16).unsqueeze(2), eq[:, :, 0:1], eq[:, :, 1:2],
                                               ALU.add))
                    dst = top(K_IDX, 512).rearrange("p (n c) -> p n c", n=2)[:, :, bass.ds(i * 16, 16)]
                    g.tensor_copy(dst, top(K_PRES, 32).rearrange("p (n c) -> p n c", n=2)).then_inc(decode_done, 1)
                    s.clear()


def to_stream(w):
    depth, rows, cols = w.shape
    assert rows == D
    return w.reshape(depth, KD, P, cols // P, P).transpose(0, 3, 2, 1, 4).reshape(depth, cols // P, P, CH)


def kernel(x, c, positions, ada_w, ada_b, norm1_g, w_in, swa_sinks, w_branch_swa, w_branch_sb,
           w_out, norm2_g, peer_wq, peer_subkeys, peer_u, peer_v, final_g):
    import concourse.bacc as bacc
    from concourse.bass_utils import run_bass_kernel_spmd as run

    arr = np.asarray
    x, c, positions = arr(x), arr(c), arr(positions)
    w_in, ada_w, ada_b = arr(w_in), arr(ada_w), arr(ada_b)
    depth = w_in.shape[0]
    f32 = np.float32

    heads = np.arange(8).reshape(2, 4).T.ravel()
    swa_cols = (heads[:, None] * HD + np.arange(HD)[None, :]).ravel()
    off = np.cumsum([0, 512, 128, 128, 512, 512, 512, 1024, 1024])
    qa, ka, va, qb, kb, vb, ga, gb = [np.arange(off[n], off[n + 1]) for n in range(8)]
    order = np.concatenate([qa[swa_cols], qb, kb, ka, va, vb])
    gates = np.concatenate([ga, gb])

    def columns(v, n):
        return arr(v).reshape(depth, n, P).transpose(0, 2, 1)

    stream = np.zeros((depth, CHUNKS, P, CH), f32)
    stream[:, 0, :, 0:48] = columns(ada_b, 48)
    stream[:, 0, :, 48:56] = columns(norm1_g, KD)
    stream[:, 0, :, 56:64] = columns(norm2_g, KD)
    stream[:, 0, :, 64:72] = arr(swa_sinks)[:, None, :]
    sub = arr(peer_subkeys).reshape(depth, 2, 8, P, P).transpose(0, 1, 4, 2, 3)
    stream[:, 1:3] = sub.reshape(depth, 2, P, CH)
    stream[:, N_PAR:M0] = to_stream(ada_w)
    branch = np.concatenate([arr(w_branch_swa)[:, swa_cols], arr(w_branch_sb)], 1)
    for m, w in ((M_QK, w_in[:, :, order]), (M_G, w_in[:, :, gates]), (M_BR, branch),
                 (M_OUT, arr(w_out)), (M_WQ, arr(peer_wq))):
        s = to_stream(w)
        stream[:, M0 + m:M0 + m + s.shape[1]] = s
    u = arr(peer_u).reshape(depth, P, P, KD, P)
    stream[:, M0 + M_U:M0 + M_VV] = u.transpose(0, 2, 4, 3, 1).reshape(depth, N_U, P, CH)
    stream[:, M0 + M_VV:] = arr(peer_v).reshape(depth, P, P, D).transpose(0, 2, 1, 3)

    arrays = {
        "consts": constants(),
        "stream": stream.reshape(depth * CHUNKS, P, CH),
        "xT": np.ascontiguousarray(x[0].reshape(T, KD, P).transpose(2, 1, 0).reshape(P, KD * T)),
        "cT": np.ascontiguousarray(c[0].reshape(KD, P).T),
        "pos": np.ascontiguousarray(np.broadcast_to(positions, (P, T))).astype(np.int32),
        "final_g": np.ascontiguousarray(arr(final_g).reshape(KD, P).T),
    }
    nc = bacc.Bacc("TRN2", target_bir_lowering=False, num_devices=1, dynamic_dma_scratch_size=64)
    aps = [nc.dram_tensor(k, v.shape, mybir.dt.from_np(v.dtype), kind="ExternalInput").ap()
           for k, v in arrays.items()]
    out = nc.dram_tensor("outT", (P, KD * T), F32, kind="ExternalOutput").ap()
    build(nc, depth, *aps, out)
    got = run(nc, [arrays], core_ids=[0]).results[0]["outT"]
    return got.reshape(P, KD, T).transpose(2, 1, 0).reshape(1, T, D)
```

```python
from contextlib import ExitStack

import numpy as np

import concourse.bass as bass
from concourse import mybir

F32 = mybir.dt.float32
F32R = mybir.dt.float32r
I32 = mybir.dt.int32
U32 = mybir.dt.uint32
ACT = mybir.ActivationFunctionType
ALU = mybir.AluOpType
AX = mybir.AxisListType

P = 128
D = 1024
KD = D // P
T = 256
TT = T // P
HD = 64
CH = KD * P
RAW = 4
W = 4
AHEAD = 3

N_QK, N_V, N_PAD, N_G, N_BR, N_OUT, N_WQ, N_U, N_VV = 13, 5, 2, 16, 8, 8, 16, 128, 128
SPLITS = N_QK + N_V + N_PAD + N_G + N_BR + N_OUT + N_WQ + N_U + N_VV
N_ADA, N_ADA1 = 48, 16
N_ADA2 = N_ADA - N_ADA1
ADA_LOADS = (N_ADA2 // 2 + N_ADA1, N_ADA2 // 2)
M_QK = 0
M_V = M_QK + N_QK
M_PAD = M_V + N_V
M_G = M_PAD + N_PAD
M_BR = M_G + N_G
M_OUT = M_BR + N_BR
M_WQ = M_OUT + N_OUT
M_U = M_WQ + N_WQ
M_VV = M_U + N_U
assert SPLITS % RAW == 0 and M_G % W == 0 and M_U % W == 0

E_QKVG = 0
E_WQ = E_QKVG + N_QK + N_V + N_G
E_SK = E_WQ + N_WQ
E_U = E_SK + 8
EVACS = E_U + N_U // 2
assert EVACS % 2 == 0

HALF = 64
GT = 8
GS = GT // 2
NG = T // GT
ITERS = HALF // 4
LAST_HEAD = [5, 6, 7, 8, 10, 12, 14, 16]
UNITS = 16

C_ID, C_TRI, C_ROT = 0, 128, 256
C_SWB = 384
C_SBM = C_SWB + 384
C_ONE = C_SBM + P
C_IOTA = C_SBM + T
C_MISC = C_IOTA + 128
NCONST = C_MISC + 4

B_QK = 0
B_VT = B_QK + 13 * T
B_GT = B_VT + TT * 640
B_Y = B_GT + 16 * T
B_MG = B_Y + KD * T
B_AT = B_MG + KD * T
RU = 8
B_SQ = B_GT
B_H = B_Y
HB = HALF * T
B_QP = HB
B_SKV = B_QP + 16 * T
B_TK = B_SKV + 16 * 256
B_SUB = 2 * HB - 16 * P
B_RSTD = B_SUB - T
B_ADA = B_RSTD - 2 * CH
B_ADA0 = B_ADA - N_ADA1 * CH
K_CUR, K_CUT, K_VAL, K_CAND, K_CCUT, K_REC, K_BEST8, K_POS = 0, 256, 512, 544, 800, 1056, 1120, 1136
K_BEST = 1152
K_RECS = K_BEST + 256
K_IDX = K_RECS + 16 * 64
K_PREC = K_IDX + 768
K_PEQ = K_PREC + 64
K_PRES = K_PEQ + 256
K_EXP = K_PRES + 32
K_SUM = K_EXP + 256
assert B_H + KD * T <= B_ADA0 and B_AT + RU * 4 * 384 <= B_ADA and B_TK + K_SUM + 32 <= B_ADA

NEG = -1e30
LOWEST = -3.0e38
TWO_PI_1 = 6.28125
TWO_PI_2 = float(np.float32(2 * np.pi - TWO_PI_1) // 2 ** -19 * 2 ** -19)
TWO_PI_3 = float(2 * np.pi - TWO_PI_1 - TWO_PI_2)
PI_DOWN = 3.1415925
ROUND = 12582912.0


def constants():
    c = np.zeros((P, NCONST), np.float32)
    a = np.arange(P)
    c[:, C_ID:C_ID + P] = np.eye(P)
    c[:, C_TRI:C_TRI + P] = a[:, None] >= a[None, :]
    for d in range(P):
        lo = d % HD < HD // 2
        c[d + HD // 2 if lo else d - HD // 2, C_ROT + d] = -1.0 if lo else 1.0
    q, k = a[:, None], a[None, :]
    c[:, C_SWB:C_SWB + P] = np.where(k <= q, 0.0, NEG)
    diff = q + P - np.arange(T)[None, :]
    c[:, C_SWB + P:C_SWB + P + T] = np.where((diff >= 0) & (diff < 128), 0.0, NEG)
    c[:, C_SBM:C_SBM + T] = a[:, None] < np.arange(T)[None, :]
    c[:, C_IOTA:C_IOTA + P] = a[None, :]
    half = HD // 2
    inv = np.power(np.float32(10000.0), -np.arange(half, dtype=np.float32) * np.float32(2.0 / HD))
    c[:, C_MISC] = inv[a % half]
    c[:, C_MISC + 1] = 1e-6
    c[:, C_MISC + 2] = 1.0
    return c



def build(nc, depth, consts, stream, ada, subkeys, params, xT, cT, pos, final_g, outT):
    with ExitStack() as ctx:
        def sb(name, shape, dt=F32):
            return ctx.enter_context(nc.sbuf_tensor(name, shape, dt))

        def sem(name):
            return ctx.enter_context(nc.semaphore(name))

        big = sb("big", [P, 2 * HB])
        raw = sb("raw", [P, RAW, CH])
        wsp = sb("wsp", [P, W, 2, CH], F32R)
        hs = sb("hs", [P, 2, KD * T], F32R)
        x = sb("x", [P, KD * T])
        con = sb("con", [P, NCONST])
        cosT = sb("cosT", [P, T])
        sinT = sb("sinT", [P, T])
        selT = sb("selT", [P, 2, T])
        selg = sb("selg", [P, 2, T], F32R)
        selc = sb("selc", [P, 2, GS])
        ohi = sb("ohi", [P, 2, GS, P], F32R)
        ohj = sb("ohj", [P, 2, 2, GT, HALF], F32R)
        cact = sb("cact", [P, 2 * KD])
        par = sb("par", [P, 72])
        mod = sb("mod", [P, 48])
        modn = sb("modn", [P, N_ADA1])
        gs = sb("gs", [P, 2 * KD])
        fg = sb("fg", [P, KD])
        st = sb("st", [P, 4, 16])

        acc = ctx.enter_context(nc.psum_tensor("acc", [P, 2, 512], F32))
        pg = ctx.enter_context(nc.psum_tensor("pg", [P, 2, 512], F32))
        yac = ctx.enter_context(nc.psum_tensor("yac", [P, 4, 512], F32))

        inputs_in = sem("inputs_in")
        landed = [sem(f"landed{s}") for s in range(RAW)]
        params_in = sem("params_in")
        first_ada_in = sem("first_ada_in")
        first_ada_done = sem("first_ada_done")
        ada_in = [sem(f"ada_in{g}") for g in range(2)]
        ada_used = sem("ada_used")
        hi_done = sem("hi_done")
        split_done = sem("split_done")
        chunk_done = sem("chunk_done")
        acc_free = sem("acc_free")
        pg_free = sem("pg_free")
        cact_ready = sem("cact_ready")
        angle_done = sem("angle_done")
        rope_table = sem("rope_table")
        mod_ready = sem("mod_ready")
        sq_done = sem("sq_done")
        ssq_done = sem("ssq_done")
        std_done = sem("std_done")
        xn_done = sem("xn_done")
        src_hi = sem("src_hi")
        src_done = sem("src_done")
        rot_done = sem("rot_done")
        rope_done = sem("rope_done")
        sc_done = sem("sc_done")
        d1_done = sem("d1_done")
        a1_done = sem("a1_done")
        d2_done = sem("d2_done")
        b_done = sem("b_done")
        d3_done = sem("d3_done")
        a2_done = sem("a2_done")
        d4_done = sem("d4_done")
        av_done = sem("av_done")
        y_taken = sem("y_taken")
        sig_done = sem("sig_done")
        sk_done = sem("sk_done")
        topk_done = sem("topk_done")
        decode_done = sem("decode_done")
        gexp_in = sem("gexp_in")
        gexp_done = sem("gexp_done")
        gates_ready = sem("gates_ready")
        selT_done = sem("selT_done")
        sel_ready = sem("sel_ready")
        ohi_done = sem("ohi_done")
        ohj_done = sem("ohj_done")
        g_done = sem("g_done")
        mul_done = sem("mul_done")
        ahi_done = sem("ahi_done")
        alo_done = sem("alo_done")
        ytok_taken = sem("ytok_taken")
        yT_done = sem("yT_done")
        xT_taken = sem("xT_taken")
        out_ready = sem("out_ready")
        out_stored = sem("out_stored")
        dve_step = sem("dve_step")
        act_step = sem("act_step")
        pool_step = sem("pool_step")

        def col(base, n=1):
            return big[:, base:base + n]

        ident = con[:, C_ID:C_ID + P]
        tri = con[:, C_TRI:C_TRI + P]
        ones = con[:, C_ONE:C_ONE + P]
        rot = con[:, C_ROT:C_ROT + P]
        iota = con[:, C_IOTA:C_IOTA + P]
        iota16 = con[:, C_IOTA:C_IOTA + 16]
        invf = con[:, C_MISC:C_MISC + 1]
        eps = con[:, C_MISC + 1:C_MISC + 2]
        one = con[:, C_MISC + 2:C_MISC + 3]
        rstd = col(B_RSTD, T)
        sinks = par[:, 64:72]

        def adab(g):
            return col(B_ADA + g * CH, CH)

        def qk(c):
            return col(B_QK + c * T, T)

        def vtok(t):
            return col(B_VT + t * 640, 640)

        def att(u, b):
            return col(B_AT + ((u % RU) * 4 + b) * 384, 384)

        def top(base, n):
            return col(B_TK + base, n)

        def half_of(h):
            return big[:, h * HB:(h + 1) * HB]

        class Steps:

            def __init__(self, eng, s):
                self.eng, self.s, self.n = eng, s, 0

            def mark(self, ins):
                self.n += 1
                ins.then_inc(self.s, 1)

            def join(self):
                self.eng.wait_ge(self.s, self.n)

            def link(self, ins):
                self.mark(ins)
                self.join()

            def clear(self):
                if self.n:
                    self.join()
                    self.eng.sem_clear(self.s)
                    self.n = 0

        def nth(L, per_layer, k, i=0, per=0):
            return L * per_layer + i * per + k

        def raw_landed(eng, L, n, i=0):
            eng.wait_ge(landed[n % RAW], nth(L, SPLITS // RAW * 16, (n // RAW + 1) * 16, i, 16))

        def act_high(act, L, m, i=0):
            raw_landed(act, L, m, i)
            act.wait_ge(chunk_done, nth(L, SPLITS, m + 1, i, 4))
            n = P if M_PAD <= m < M_G and isinstance(i, int) else CH
            nc.scalar.activation(wsp[:, m % W, 0, 0:n], raw[:, m % RAW, 0:n],
                                 ACT.Copy).then_inc(hi_done, 1)

        def dve_low(dve, L, m, i=0):
            dve.wait_ge(hi_done, nth(L, SPLITS, m + 1, i, 4))
            n = P if M_PAD <= m < M_G and isinstance(i, int) else CH
            nc.vector.tensor_tensor(wsp[:, m % W, 1, 0:n], raw[:, m % RAW, 0:n],
                                    wsp[:, m % W, 0, 0:n].bitcast(F32),
                                    ALU.subtract).then_inc(split_done, 1)

        def chunk_split(pe, L, m, i=0):
            pe.wait_ge(split_done, nth(L, SPLITS, m + 1, i, 4))

        def chunk_used(eng, L, m, i=0):
            eng.wait_ge(chunk_done, nth(L, SPLITS, W + m + 1, i, 4))

        TERMS = ((0, 1), (1, 0), (0, 0))

        def product(pe, out, m, k0=0, k1=KD):
            mm = None
            for k in range(k0, k1):
                for n, (a, b) in enumerate(TERMS):
                    mm = pe.matmul(out, wsp[:, m % W, a, k * P:(k + 1) * P], hs[:, b, k * T:(k + 1) * T],
                                   start=(k == k0 and n == 0), stop=(k == k1 - 1 and n == 2))
            return mm

        block = ctx.enter_context(nc.Block())

        @block.sync
        def _(sp):
            sp.dma_start(con[:, :], consts).then_inc(inputs_in, 16)
            sp.dma_start(x[:, :], xT).then_inc(inputs_in, 16)
            sp.dma_start(cact[:, 0:KD], cT).then_inc(inputs_in, 16)
            sp.dma_start(cosT[:, :].bitcast(I32), pos).then_inc(inputs_in, 16)
            sp.dma_start(fg[:, :], final_g).then_inc(inputs_in, 16)

            def load(n, L=0, i=0):
                src = stream[bass.ds(nth(L, SPLITS, n, i, 4), 1), :, :]
                sp.dma_start(raw[:, n % RAW, :], src.rearrange("a p c -> p (a c)")).then_inc(landed[n % RAW], 16)

            def load_ada(L, a, i=0, per=0):
                g = a % 2
                src = ada[bass.ds(nth(L, N_ADA, N_ADA1 + a, i, per), 1), :, :]
                sp.dma_start(adab(g), src.rearrange("a p c -> p (a c)")).then_inc(ada_in[g], 16)

            def steps(L, n, i=0):
                for c in range(4):
                    sp.wait_ge(split_done, nth(L, SPLITS, n + c - RAW + 1, i, 4))
                    load(n + c, L, i)
                    yield c

            for a in range(N_ADA1):
                sp.dma_start(col(B_ADA0 + a * CH, CH), ada[a, :, :]).then_inc(first_ada_in, 16)
            for n in range(RAW):
                sp.dma_start(raw[:, n, :], stream[n, :, :]).then_inc(landed[n], 16)
            with sp.Fori(0, depth, 1) as L:
                sp.wait_ge(xT_taken, nth(L, 4, 4))
                sp.dma_start(par[:, :], params[bass.ds(L, 1), :, :].rearrange("a p c -> p (a c)")).then_inc(
                    params_in, 16)
                sp.dma_start(col(B_SUB, 2 * CH), subkeys[bass.ds(L, 1), :, :].rearrange("a p c -> p (a c)")).then_inc(
                    params_in, 16)
                with sp.Fori(0, N_ADA2 // 4, 1) as i:
                    for c in steps(L, RAW, i):
                        sp.wait_ge(ada_used, nth(L, N_ADA, c + 1, i, 4))
                        load_ada(L, c, i, 4)
                with sp.Fori(0, (M_U - RAW - N_ADA2) // 4, 1) as i:
                    for c in steps(L, RAW + N_ADA2, i):
                        pass
                with sp.Fori(0, ITERS, 1) as i:
                    for c in steps(L, M_U, i):
                        pass
                    sp.wait_ge(ada_used, nth(L, N_ADA, 2 + N_ADA2, i, 1))
                    load_ada(L, N_ADA2, i, 1)
                with sp.Fori(0, (SPLITS + RAW - M_U - HALF) // 4, 1) as i:
                    for c in steps(L, M_U + HALF, i):
                        pass
            sp.wait_ge(out_ready, KD)
            sp.dma_start(outT, col(B_H, KD * T)).then_inc(out_stored, 16)
            sp.wait_ge(out_stored, 16)

        @block.tensor
        def _(pe):
            pe.sem_inc(chunk_done, W)
            pe.sem_inc(ada_used, 2)
            pe.sem_inc(g_done, 2)

            def ssq(n, count):
                pe.wait_ge(sq_done, count)
                for k in range(KD):
                    mm = pe.matmul(yac[:, 1, 0:T], ones, col(B_SQ + k * T, T),
                                   start=(k == 0), stop=(k == KD - 1))
                mm.then_inc(ssq_done, 1)

            def ada_product(out, w):
                for k in range(KD):
                    mm = pe.matmul(out, w[:, k * P:(k + 1) * P], cact[:, KD + k:KD + k + 1],
                                   start=(k == 0), stop=(k == KD - 1), skip_group_check=True)
                return mm

            def ada_beside(L, e, i=0):
                if e < N_ADA2:
                    pe.wait_ge(ada_in[e % 2], nth(L, ADA_LOADS[e % 2] * 16, (e // 2 + 1) * 16, i, 32))
                    ada_product(acc[:, e % 2, T:T + 1], adab(e % 2)).then_inc(ada_used, 1)

            def by_features(L, m, e, i=0):
                pe.wait_ge(acc_free, nth(L, EVACS, e + 1, i, 4))
                ada_beside(L, e, i)
                chunk_split(pe, L, m, i)
                product(pe, acc[:, e % 2, 0:T], m).then_inc(chunk_done, 1)

            def by_tokens(L, m, e):
                pe.wait_ge(acc_free, nth(L, EVACS, e + 1))
                ada_beside(L, e)
                chunk_split(pe, L, m)
                for t in range(TT):
                    for k in range(KD):
                        for n, (a, b) in enumerate(TERMS):
                            mm = pe.matmul(acc[:, e % 2, t * P:(t + 1) * P],
                                           hs[:, b, k * T + t * P:k * T + (t + 1) * P],
                                           wsp[:, m % W, a, k * P:(k + 1) * P],
                                           start=(k == 0 and n == 0), stop=(k == KD - 1 and n == 2))
                mm.then_inc(chunk_done, 1)

            def rotate(L, n):
                c = n if n < 4 else 12
                e = E_QKVG + c
                pe.wait_ge(acc_free, nth(L, EVACS, e + 3))
                out = pg[:, n // 2, n % 2 * T:(n % 2 + 1) * T] if n < 4 else yac[:, 0, 0:T]
                pe.matmul(out, rot, qk(c), start=True, stop=True).then_inc(rot_done, 1)

            def head_scores(L, u):
                out = pg[:, u % 2, :]
                if u < 2:
                    pe.wait_ge(rope_done, nth(L, 5, 5))
                if u >= 2:
                    pe.wait_ge(d1_done, nth(L, UNITS, u - 1))
                if u < 8:
                    b, q, k = HD * (u // 4), qk(u % 4), qk(12)
                    pe.matmul(out[:, 0:P], q[b:b + HD, 0:P], k[b:b + HD, 0:P], start=True, stop=True)
                    mm = pe.matmul(out[:, P:384], q[b:b + HD, P:T], k[b:b + HD, 0:T], start=True, stop=True)
                else:
                    h = u - 8
                    b, q, k = HD * (h % 2), qk(4 + h // 2), qk(8 + h // 2)
                    pe.matmul(out[:, 0:T], k[b:b + HD, 0:P], q[b:b + HD, 0:T], start=True, stop=True)
                    mm = pe.matmul(out[:, T:384], k[b:b + HD, P:T], q[b:b + HD, P:T], start=True, stop=True)
                mm.then_inc(sc_done, 1)

            def head_middle(L, u):
                out = yac[:, u % 2, :]
                pe.wait_ge(d2_done, nth(L, UNITS, u + 1))
                if 2 <= u < 10:
                    pe.wait_ge(a2_done, nth(L, UNITS, u - 1))
                elif u >= 10:
                    pe.wait_ge(d3_done, nth(L, 8, u - 9))
                if u < 8:
                    for j in range(3):
                        mm = pe.transpose(out[:, j * P:(j + 1) * P], att(u, 1)[:, j * P:(j + 1) * P], ident)
                else:
                    s = att(u, 3)
                    pe.matmul(out[:, 0:T], tri, s[:, 0:T], start=True, stop=False, skip_group_check=True)
                    pe.matmul(out[:, P:T], ones, s[:, T:384], start=False, stop=True, skip_group_check=True)
                    mm = pe.matmul(out[:, T:384], tri, s[:, T:384], start=True, stop=True, skip_group_check=True)
                mm.then_inc(b_done, 1)

            def head_values(L, u):
                if u < 8:
                    pe.wait_ge(a2_done, nth(L, UNITS, u + 1))
                    b, vc = HD * (u // 4), HD * (u // 4)
                else:
                    h = u - 8
                    pe.wait_ge(d4_done, nth(L, 8, h + 1))
                    b, vc = HD * (h % 2), P + HD * h
                w = att(u, 2)
                if u >= 2:
                    pe.wait_ge(y_taken, nth(L, UNITS, u - 1))
                out = yac[b:b + HD, 2 + u % 2, :]
                pe.matmul(out[:, 0:T], vtok(0)[:, vc:vc + HD], w[:, 0:T], start=True, stop=False,
                          skip_group_check=True)
                pe.matmul(out[:, P:T], vtok(1)[:, vc:vc + HD], w[:, T:384], start=False, stop=True,
                          skip_group_check=True).then_inc(av_done, 1)

            def gate_matrices(L, half, s, i):
                g, b = s // 2 % 2, s % 2
                pe.wait_ge(ohi_done, nth(L, 4 * NG, 2 * half * NG + s + 1, i, 4))
                if b == 0:
                    k = half * NG + s // 2
                    pe.wait_ge(ohj_done, nth(L, 2 * NG, k + 1, i, 2))
                    pe.wait_ge(mul_done, nth(L, 2 * NG, k + 1, i, 2))
                for t in range(GS):
                    for a in (1, 0):
                        mm = pe.matmul(pg[:, g, (b * GS + t) * HALF:(b * GS + t + 1) * HALF], ohi[:, b, t, :],
                                       ohj[:, g, a, b * GS + t, :], start=(a == 1), stop=(a == 0))
                mm.then_inc(g_done, 1)

            def expert_pair(L, half, c, i, gates=False):
                m = M_U + half * HALF + c
                e = E_U + (half * HALF + c) // 2
                for a in range(2):
                    if gates:
                        gate_matrices(L, 0, c + a, i)
                    if a == 0:
                        pe.wait_ge(acc_free, nth(L, EVACS, e + 1, i, 2))
                    chunk_split(pe, L, m + a, i)
                    product(pe, acc[:, e % 2, a * T:(a + 1) * T], m + a).then_inc(chunk_done, 1)

            def value_chunk(L, half, c, i, start=False, stop=False):
                m = M_VV + half * HALF + c
                if c % 2 == 0:
                    pe.wait_ge(alo_done, nth(L, HALF, (half * HALF + c) // 2 + 1, i, 2))
                chunk_split(pe, L, m, i)
                for t in range(TT):
                    for n, (a, b) in enumerate(TERMS):
                        for w in range(2):
                            mm = pe.matmul(yac[:, 2 * t + w, :], hs[:, b, c * T + t * P:c * T + (t + 1) * P],
                                           wsp[:, m % W, a, w * 512:(w + 1) * 512],
                                           start=(start and n == 0), stop=(stop and n == 2),
                                           skip_group_check=True)
                mm.then_inc(chunk_done, 1)

            pe.wait_ge(inputs_in, 80)
            pe.wait_ge(cact_ready, 1)
            pe.wait_ge(first_ada_in, 16 * N_ADA1)
            for a in range(N_ADA1):
                mm = ada_product(yac[:, 0, a:a + 1], col(B_ADA0 + a * CH, CH))
            mm.then_inc(first_ada_done, 1)
            with pe.Fori(0, depth, 1) as L:
                ssq(0, nth(L, 2, 1))
                with pe.Fori(0, 3, 1) as i:
                    pe.wait_ge(src_done, nth(L, 4 * KD, KD))
                    for c in range(4):
                        by_features(L, M_QK + c, E_QKVG + c, i)
                by_features(L, M_QK + 12, E_QKVG + 12)
                for c in range(N_V):
                    by_tokens(L, M_V + c, E_QKVG + N_QK + c)
                for m in range(M_PAD, M_G):
                    chunk_split(pe, L, m)
                    pe.matmul(yac[:, 2, 0:2], wsp[:, m % W, 0, 0:P], wsp[:, m % W, 1, 0:2],
                              start=True, stop=True).then_inc(chunk_done, 1)
                for n in range(5):
                    rotate(L, n)
                for s in range(UNITS + 5):
                    if s < N_G:
                        by_features(L, M_G + s, E_QKVG + N_QK + N_V + s)
                    if s < UNITS:
                        head_scores(L, s)
                    if 2 <= s < UNITS + 2:
                        head_middle(L, s - 2)
                    if 4 <= s < UNITS + 4:
                        head_values(L, s - 4)
                with pe.Fori(0, N_BR // 4, 1) as i:
                    pe.wait_ge(src_done, nth(L, 4 * KD, 2 * KD))
                    for c in range(4):
                        chunk_split(pe, L, M_BR + c, i)
                        pe.wait_ge(pg_free, nth(L, N_BR + N_OUT, c + 1, i, 4))
                        product(pe, pg[:, c % 2, 0:T], M_BR + c, 0, 4)
                        product(pe, pg[:, c % 2, T:2 * T], M_BR + c, 4, 8).then_inc(chunk_done, 1)
                with pe.Fori(0, N_OUT // 4, 1) as i:
                    pe.wait_ge(src_done, nth(L, 4 * KD, 3 * KD))
                    for c in range(4):
                        chunk_split(pe, L, M_OUT + c, i)
                        pe.wait_ge(pg_free, nth(L, N_BR + N_OUT, N_BR + c + 1, i, 4))
                        product(pe, pg[:, c % 2, 0:T], M_OUT + c).then_inc(chunk_done, 1)
                ssq(1, nth(L, 2, 2))
                with pe.Fori(0, N_WQ // 4, 1) as i:
                    pe.wait_ge(src_done, nth(L, 4 * KD, 4 * KD))
                    for c in range(4):
                        by_features(L, M_WQ + c, E_WQ + c, i)
                pe.wait_ge(params_in, nth(L, 32, 32))
                for e in range(8):
                    t, q = e // 4, e % 4
                    pe.wait_ge(acc_free, nth(L, EVACS, E_SK + e + 1 if e > 1 else E_SK + 2))
                    for n in range(4):
                        mm = pe.matmul(acc[:, e % 2, n * P:(n + 1) * P],
                                       col(B_QP + (4 * q + n) * T + t * P, P),
                                       col(B_SUB + (4 * q + n) * P, P), start=True, stop=True)
                    mm.then_inc(sk_done, 1)
                with pe.Fori(0, ITERS, 1) as i:
                    expert_pair(L, 0, 0, i)
                    pe.wait_ge(ada_in[0], nth(L, ADA_LOADS[0] * 16, (N_ADA2 // 2 + 1) * 16, i, 16))
                    ada_product(yac[:, 0, bass.ds(i, 1)], adab(0)).then_inc(ada_used, 1)
                    expert_pair(L, 0, 2, i)
                pe.wait_ge(gates_ready, nth(L, 1, 1))
                for t in range(TT):
                    for n in range(3):
                        mm = pe.transpose(pg[:, t, n * P:(n + 1) * P], top(K_IDX + n * T + t * P, P), ident)
                mm.then_inc(selT_done, 1)
                with pe.Fori(0, ITERS, 1) as i:
                    for g in range(2):
                        expert_pair(L, 1, 2 * g, i, gates=True)

                def values_and_gates(i, start=False):
                    for c in range(4):
                        gate_matrices(L, 1, c, i)
                        value_chunk(L, 0, c, i, start=start and c == 0)

                values_and_gates(0, start=True)
                with pe.Fori(1, ITERS, 1) as i:
                    values_and_gates(i)
                with pe.Fori(0, ITERS - 1, 1) as i:
                    for c in range(4):
                        value_chunk(L, 1, c, i)
                for c in range(4):
                    value_chunk(L, 1, c, ITERS - 1, stop=(c == 3))
                pe.wait_ge(ytok_taken, nth(L, 1, 1))
                for g in range(4):
                    out = acc[:, g, :] if g < 2 else pg[:, g - 2, :]
                    for k in range(2):
                        for t in range(TT):
                            mm = pe.transpose(out[:, k * T + t * P:k * T + (t + 1) * P],
                                              col(t * D + (2 * g + k) * P, P), ident)
                    mm.then_inc(yT_done, 1)
            ssq(2, 2 * depth + 1)

        @block.scalar
        def _(act):
            a = Steps(act, act_step)
            act.sem_inc(acc_free, 2)
            nc_act = nc.scalar

            def rms(count):
                nc_act.activation(col(B_SQ, KD * T), x[:, :], ACT.Square).then_inc(sq_done, 1)
                act.wait_ge(ssq_done, count)
                nc_act.activation(rstd, yac[:, 1, 0:T], ACT.Sqrt, bias=eps,
                                  scale=1.0 / D).then_inc(std_done, 1)

            def modulated(L, w):
                for k in range(KD):
                    act.wait_ge(xn_done, nth(L, 2 * KD, w * KD + k + 1))
                    h = col(B_H + k * T, T)
                    a.link(nc_act.activation(h, h, ACT.Identity, bias=mod[:, 24 * w + k:24 * w + k + 1],
                                             scale=gs[:, KD * w + k:KD * w + k + 1]))
                    nc_act.activation(hs[:, 0, k * T:(k + 1) * T], h, ACT.Copy).then_inc(src_hi, 1)

            def store_mod(e, i=0):
                if e < N_ADA2:
                    nc_act.activation(mod[:, bass.ds(nth(i, 4, N_ADA1 + e), 1)], acc[:, e % 2, T:T + 1], ACT.Copy)

            def store(L, m, e, dst, i=0):
                chunk_used(act, L, m, i)
                store_mod(e, i)
                nc_act.activation(dst, acc[:, e % 2, 0:T], ACT.Copy).then_inc(acc_free, 1)

            def head_a1(L, u):
                act.wait_ge(d1_done, nth(L, UNITS, u + 1))
                s = st[:, u % 4, :]
                if u < 8:
                    for b in range(2):
                        lo, hi = (0, P) if b == 0 else (P, 384)
                        nc_act.activation(att(u, 1)[:, lo:hi], att(u, 0)[:, lo:hi], ACT.Exp,
                                          bias=s[:, 2 + b:3 + b], accum_out=s[:, 4 + b:5 + b])
                    nc_act.activation(s[:, 6:8], s[:, 2:4], ACT.Exp,
                                      bias=sinks[:, u:u + 1]).then_inc(a1_done, 1)
                else:
                    a.link(nc_act.activation(att(u, 1), att(u, 0), ACT.Abs))
                    a.link(nc_act.activation(att(u, 2), att(u, 1), ACT.Exp, scale=-1.0))
                    nc_act.activation(att(u, 1), att(u, 2), ACT.Ln, bias=one).then_inc(a1_done, 1)

            def head_a2(L, u):
                if u < 8:
                    act.wait_ge(b_done, nth(L, UNITS, u + 1))
                    nc_act.activation(att(u, 2), yac[:, u % 2, 0:384], ACT.Copy).then_inc(a2_done, 1)
                else:
                    act.wait_ge(d3_done, nth(L, 8, u - 8 + 1))
                    nc_act.activation(att(u, 1), att(u, 3), ACT.Exp).then_inc(a2_done, 1)

            def gelu_pair(L, half, c, i):
                m = M_U + half * HALF + c
                e = E_U + (half * HALF + c) // 2
                chunk_used(act, L, m + 1, i)
                nc_act.activation(half_of(half)[:, bass.ds(nth(i, 4 * T, c * T), 2 * T)],
                                  acc[:, e % 2, :], ACT.Gelu).then_inc(acc_free, 1)

            def a_high(L, half, q, i):
                r = half * (HALF // 2) + q
                if q > 1 or not isinstance(i, int) or i:
                    chunk_used(act, L, M_VV + 2 * r - 3, i)
                nc_act.activation(hs[:, 0, q % 2 * 2 * T:(q % 2 + 1) * 2 * T],
                                  half_of(half)[:, bass.ds(nth(i, 4 * T, 2 * q * T), 2 * T)],
                                  ACT.Copy).then_inc(ahi_done, 1)

            act.wait_ge(inputs_in, 80)
            nc_act.activation(cact[:, KD:2 * KD], cact[:, 0:KD], ACT.Silu).then_inc(cact_ready, 1)
            act.wait_ge(angle_done, 1)
            nc_act.activation(sinT[:, :], qk(0), ACT.Sin)
            nc_act.activation(cosT[:, :], qk(1), ACT.Sin).then_inc(rope_table, 1)
            with act.Fori(0, depth, 1) as L:
                act.wait_ge(xT_taken, nth(L, 4, 4))
                rms(nth(L, 2, 1))
                for m in range(AHEAD):
                    act_high(act, L, m)
                act.wait_ge(mod_ready, nth(L, 1, 1))
                modulated(L, 0)
                a.clear()
                with act.Fori(0, 3, 1) as i:
                    for c in range(4):
                        act_high(act, L, M_QK + c + AHEAD, i)
                        store(L, M_QK + c, E_QKVG + c, big[:, bass.ds(nth(i, 4 * T, B_QK + c * T), T)], i)
                act_high(act, L, M_QK + 12 + AHEAD)
                store(L, M_QK + 12, E_QKVG + 12, qk(12))
                for c in range(N_V):
                    e = E_QKVG + N_QK + c
                    act_high(act, L, M_V + c + AHEAD)
                    chunk_used(act, L, M_V + c)
                    store_mod(e)
                    dst = col(B_VT, TT * 640).rearrange("p (t f) -> p t f", t=TT)[:, :, c * P:(c + 1) * P]
                    nc_act.activation(dst, acc[:, e % 2, 0:T].rearrange("p (t f) -> p t f", t=TT),
                                      ACT.Copy).then_inc(acc_free, 1)
                for m in range(M_PAD, M_G):
                    act_high(act, L, m + AHEAD)
                act.preload_act_table_set("natural_log_exp_and_others")
                for s in range(UNITS + 5):
                    if s < N_G:
                        act_high(act, L, M_G + s + AHEAD)
                    if 1 <= s <= N_G:
                        store(L, M_G + s - 1, E_QKVG + N_QK + N_V + s - 1, col(B_GT + (s - 1) * T, T))
                    if 1 <= s < UNITS + 1:
                        head_a1(L, s - 1)
                    if 3 <= s < UNITS + 3:
                        head_a2(L, s - 3)
                for k in range(KD):
                    if k == 0:
                        chunk_used(act, L, M_G + N_G - 1)
                    act.wait_ge(y_taken, nth(L, UNITS, LAST_HEAD[k]))
                    nc_act.activation(hs[:, 0, k * T:(k + 1) * T], col(B_Y + k * T, T),
                                      ACT.Copy).then_inc(src_hi, 1)
                act.wait_ge(acc_free, nth(L, EVACS, E_WQ + 2))
                nc_act.activation(col(B_GT, 16 * T), col(B_GT, 16 * T), ACT.Sigmoid).then_inc(sig_done, 1)
                a.clear()
                with act.Fori(0, N_BR // 4, 1) as i:
                    for c in range(4):
                        act_high(act, L, M_BR + c + AHEAD, i)
                chunk_used(act, L, M_BR + N_BR - 1)
                for k in range(KD):
                    act.wait_ge(pg_free, nth(L, N_BR + N_OUT, 2 + k + 1))
                    nc_act.activation(hs[:, 0, k * T:(k + 1) * T], col(B_MG + k * T, T),
                                      ACT.Copy).then_inc(src_hi, 1)
                with act.Fori(0, N_OUT // 4, 1) as i:
                    for c in range(4):
                        act_high(act, L, M_OUT + c + AHEAD, i)
                act.wait_ge(pg_free, nth(L, N_BR + N_OUT, 2 + N_BR + N_OUT))
                rms(nth(L, 2, 2))
                modulated(L, 1)
                a.clear()
                with act.Fori(0, N_WQ // 4, 1) as i:
                    for c in range(4):
                        act_high(act, L, M_WQ + c + AHEAD, i)
                        store(L, M_WQ + c, E_WQ + c, big[:, bass.ds(nth(i, 4 * T, B_QP + c * T), T)], i)
                for e in range(8):
                    act.wait_ge(sk_done, nth(L, 8, e + 1))
                    nc_act.activation(col(B_SKV + e * 512, 512), acc[:, e % 2, :],
                                      ACT.Copy).then_inc(acc_free, 1)
                act.preload_act_table(ACT.Gelu)
                with act.Fori(0, ITERS, 1) as i:
                    for c in (0, 2):
                        act_high(act, L, M_U + c + AHEAD, i)
                        act_high(act, L, M_U + c + 1 + AHEAD, i)
                        gelu_pair(L, 0, c, i)
                act.wait_ge(gexp_in, nth(L, 1, 1))
                nc_act.activation(top(K_EXP, 256), top(K_EXP, 256), ACT.Exp).then_inc(gexp_done, 1)
                act.preload_act_table(ACT.Gelu)
                act.wait_ge(selT_done, nth(L, 1, 1))
                with act.Fori(0, ITERS, 1) as i:
                    for c in (0, 2):
                        act_high(act, L, M_U + HALF + c + AHEAD, i)
                        act_high(act, L, M_U + HALF + c + 1 + AHEAD, i)
                        gelu_pair(L, 1, c, i)

                def values(half, i, last=False, end=False):
                    for q in range(2):
                        if not (last and q == 1):
                            a_high(L, half, q + 1, i)
                        for c in (2 * q, 2 * q + 1):
                            if not (end and c + AHEAD >= 4):
                                act_high(act, L, M_VV + half * HALF + c + AHEAD, i)

                act.wait_ge(mul_done, nth(L, 2 * NG, 2 + NG))
                a_high(L, 0, 0, 0)
                with act.Fori(0, ITERS - 1, 1) as i:
                    values(0, i)
                values(0, ITERS - 1, last=True)
                act.wait_ge(mul_done, nth(L, 2 * NG, 2 + 2 * NG))
                chunk_used(act, L, M_VV + HALF - 3)
                a_high(L, 1, 0, 0)
                with act.Fori(0, ITERS - 1, 1) as i:
                    values(1, i)
                values(1, ITERS - 1, last=True, end=True)
                a.clear()
            act.wait_ge(xT_taken, 4 * depth + 4)
            rms(2 * depth + 1)
            for k in range(KD):
                act.wait_ge(xn_done, 2 * KD * depth + k + 1)
                h = col(B_H + k * T, T)
                nc_act.activation(h, h, ACT.Copy, scale=fg[:, k:k + 1]).then_inc(out_ready, 1)

        @block.vector
        def _(dve):
            v = nc.vector
            d = Steps(dve, dve_step)
            dve.sem_inc(pg_free, 2)
            dve.sem_inc(mul_done, 2)
            dve.sem_inc(xT_taken, 4)

            def normalised(n, count):
                dve.wait_ge(std_done, count)
                d.link(v.reciprocal(rstd, rstd))
                for k in range(KD):
                    v.tensor_tensor(col(B_H + k * T, T), x[:, k * T:(k + 1) * T], rstd,
                                    ALU.mult).then_inc(xn_done, 1)

            def source_low(L, s, src):
                for k in range(KD):
                    dve.wait_ge(src_hi, nth(L, 4 * KD, s * KD + k + 1))
                    v.tensor_tensor(hs[:, 1, k * T:(k + 1) * T], col(src + k * T, T),
                                    hs[:, 0, k * T:(k + 1) * T].bitcast(F32),
                                    ALU.subtract).then_inc(src_done, 1)

            def rope(L, n):
                c = n if n < 4 else 12
                dve.wait_ge(rot_done, nth(L, 5, n // 2 * 2 + 2 if n < 4 else 5))
                r = pg[:, n // 2, n % 2 * T:(n % 2 + 1) * T] if n < 4 else yac[:, 0, 0:T]
                d.mark(v.tensor_tensor(att(n, 0)[:, 0:T], r, sinT[:, :], ALU.mult))
                d.link(v.tensor_tensor(qk(c), qk(c), cosT[:, :], ALU.mult))
                v.tensor_tensor(qk(c), qk(c), att(n, 0)[:, 0:T], ALU.add).then_inc(rope_done, 1)

            def head_d1(L, u):
                dve.wait_ge(sc_done, nth(L, UNITS, u + 1))
                z, s = pg[:, u % 2, 0:384], st[:, u % 4, :]
                if u < 8:
                    d.link(v.scalar_tensor_tensor(att(u, 0), z, HD ** -0.5, con[:, C_SWB:C_SWB + 384],
                                                  ALU.mult, ALU.add))
                    d.mark(v.tensor_reduce(s[:, 0:1], att(u, 0)[:, 0:P], AX.X, ALU.max))
                    d.link(v.tensor_reduce(s[:, 1:2], att(u, 0)[:, P:384], AX.X, ALU.max))
                    v.tensor_scalar(s[:, 2:4], s[:, 0:2], sinks[:, u:u + 1], -1.0, ALU.max,
                                    ALU.mult).then_inc(d1_done, 1)
                else:
                    v.scalar_tensor_tensor(att(u, 0)[:, 0:T], z[:, 0:T], HD ** -0.5,
                                           con[:, C_SBM:C_SBM + T], ALU.mult, ALU.mult)
                    v.scalar_tensor_tensor(att(u, 0)[:, T:384], z[:, T:384], HD ** -0.5,
                                           con[:, C_SBM:C_SBM + P], ALU.mult, ALU.mult).then_inc(d1_done, 1)

            def masked(dst, src):
                v.tensor_tensor(dst[:, 0:T], src[:, 0:T], con[:, C_SBM:C_SBM + T], ALU.mult)
                return v.tensor_tensor(dst[:, T:384], src[:, T:384], con[:, C_SBM:C_SBM + P], ALU.mult)

            def head_d2(L, u):
                dve.wait_ge(a1_done, nth(L, UNITS, u + 1))
                s = st[:, u % 4, :]
                if u < 8:
                    d.link(v.tensor_tensor(s[:, 8:10], s[:, 4:6], s[:, 6:8], ALU.add))
                    d.link(v.reciprocal(s[:, 10:12], s[:, 8:10]))
                    p = att(u, 1)
                    v.tensor_scalar(p[:, 0:P], p[:, 0:P], s[:, 10:11], None, ALU.mult)
                    v.tensor_scalar(p[:, P:384], p[:, P:384], s[:, 11:12], None,
                                    ALU.mult).then_inc(d2_done, 1)
                else:
                    d.link(v.scalar_tensor_tensor(att(u, 2), att(u, 0), 0.0, att(u, 1), ALU.max, ALU.add))
                    masked(att(u, 3), att(u, 2)).then_inc(d2_done, 1)

            def head_d3(L, u):
                dve.wait_ge(b_done, nth(L, UNITS, u + 1))
                v.tensor_tensor(att(u, 3), att(u, 0), yac[:, u % 2, 0:384], ALU.subtract).then_inc(d3_done, 1)

            def head_d4(L, u):
                dve.wait_ge(a2_done, nth(L, UNITS, u + 1))
                masked(att(u, 2), att(u, 1)).then_inc(d4_done, 1)

            def head_out(L, u):
                dve.wait_ge(av_done, nth(L, UNITS, u + 1))
                h = u - 8
                b, c = (HD * (u // 4), u % 4) if u < 8 else (HD * (h % 2), 4 + h // 2)
                v.tensor_copy(col(B_Y + c * T, T)[b:b + HD, :],
                              yac[b:b + HD, 2 + u % 2, 0:T]).then_inc(y_taken, 1)

            def top16(values, cut, best, index):
                d.link(v.max(best[:, 0:8], values))
                d.mark(v.max_index(index[:, 0:8], best[:, 0:8], values))
                d.link(v.match_replace(cut, best[:, 0:8], values, LOWEST))
                d.link(v.max(best[:, 8:16], cut))
                d.link(v.max_index(index[:, 8:16], best[:, 8:16], cut))

            def subkey_topk(L, i):
                d.link(v.tensor_copy(top(K_CUR, 256), big[:, bass.ds(nth(i, 256, B_SKV), 256)]))
                for p in range(2):
                    top16(top(K_CUR + p * P, P), top(K_CUT, P), top(K_VAL + 16 * p, 16),
                          top(K_REC + 16 * p, 16).bitcast(U32))

            def pair_topk(L, i):
                cand = top(K_CAND, 256)
                shape = [P, 16, 16]
                d.link(v.tensor_tensor(cand.rearrange("p (a b) -> p a b", a=16),
                                       top(K_VAL, 16).unsqueeze(2).to_broadcast(shape),
                                       top(K_VAL + 16, 16).unsqueeze(1).to_broadcast(shape), ALU.add))
                pos_ = top(K_POS, 16).bitcast(U32)
                top16(cand, top(K_CCUT, 256), top(K_BEST8, 16), pos_)
                d.mark(v.tensor_copy(big[:, bass.ds(nth(i, 16, B_TK + K_BEST), 16)], top(K_BEST8, 16)))
                d.mark(v.tensor_scalar(top(K_REC + 32, 16).bitcast(U32), pos_, 4, None, ALU.logical_shift_right))
                d.link(v.tensor_scalar(top(K_REC + 48, 16).bitcast(U32), pos_, 15, None, ALU.bitwise_and))
                v.tensor_copy(big[:, bass.ds(nth(i, 64, B_TK + K_RECS), 64)],
                              top(K_REC, 64).bitcast(U32)).then_inc(topk_done, 1)

            shape = [P, GT, HALF]

            def mask(L, half, g, i):
                if half or g:
                    dve.wait_ge(g_done, nth(L, 4 * NG, 2 * (half * NG + g), i, 4))
                j = selT[:, 1, bass.ds(nth(i, 2 * GT, g * GT), GT)].unsqueeze(2).to_broadcast(shape)
                d.mark(v.tensor_tensor(ohj[:, g % 2, 0], iota[:, half * HALF:(half + 1) * HALF].unsqueeze(1)
                                       .to_broadcast(shape), j, ALU.is_equal))

            def mask_times(g, a, i):
                d.join()
                part = selg[:, a, bass.ds(nth(i, 2 * GT, g * GT), GT)].bitcast(F32).unsqueeze(2)
                return v.tensor_tensor(ohj[:, g % 2, a], ohj[:, g % 2, 0].bitcast(F32), part.to_broadcast(shape),
                                       ALU.mult)

            def gate(L, half, g, i, back=0):
                dve.wait_ge(g_done, nth(L, 4 * NG, 2 + 2 * (half * NG + g - back + 1), i, 4))
                dst = half_of(half).rearrange("p (j t) -> p j t", t=T)[
                    :, :, bass.ds(nth(i, 2 * GT, (g - back) * GT), GT)]
                v.tensor_tensor(dst, dst, pg[:, g, :].rearrange("p (t j) -> p j t", t=GT),
                                ALU.mult).then_inc(mul_done, 1)

            def chunks_and_gates(L, m, half, i, first=False, last=False, values=False):
                for g in range(2):
                    nh, ng, ni = (1, 0, 0) if last and g == 1 else (half, g + 1, i)
                    build_next = not (last and g == 1 and half == 1)
                    if values and not (last and g == 1):
                        a_low(L, 0, g + 1, i)
                    dve_low(dve, L, m + 2 * g + AHEAD, i)
                    if build_next:
                        mask(L, nh, ng, ni)
                    if not (first and g == 0):
                        gate(L, half, 1 - g, i, back=2 if g == 0 else 0)
                    if build_next:
                        d.mark(mask_times(ng, 1, ni))
                    dve_low(dve, L, m + 2 * g + 1 + AHEAD, i)
                    if build_next:
                        mask_times(ng, 0, ni).then_inc(ohj_done, 1)

            def a_low(L, half, q, i):
                dve.wait_ge(ahi_done, nth(L, HALF, half * HALF // 2 + q + 1, i, 2))
                s = slice(q % 2 * 2 * T, (q % 2 + 1) * 2 * T)
                v.tensor_tensor(hs[:, 1, s], half_of(half)[:, bass.ds(nth(i, 4 * T, 2 * q * T), 2 * T)],
                                hs[:, 0, s].bitcast(F32), ALU.subtract).then_inc(alo_done, 1)

            dve.wait_ge(inputs_in, 80)
            ang, cang, turns = qk(0), qk(1), qk(2)
            d.link(v.tensor_copy(cang, cosT[:, :].bitcast(I32)))
            d.link(v.tensor_scalar(ang, cang, invf, None, ALU.mult))
            d.link(v.tensor_scalar(turns, ang, 1.0 / (2 * np.pi), None, ALU.mult))
            d.link(v.tensor_scalar(turns, turns, ROUND, None, ALU.add))
            d.link(v.tensor_scalar(turns, turns, ROUND, None, ALU.subtract))
            for part in (TWO_PI_1, TWO_PI_2, TWO_PI_3):
                d.link(v.scalar_tensor_tensor(ang, turns, -part, ang, ALU.mult, ALU.add))
            d.link(v.tensor_scalar(cang, ang, np.pi / 2, None, ALU.add))
            d.link(v.tensor_scalar(turns, cang, np.pi, -2 * np.pi, ALU.is_gt, ALU.mult))
            d.link(v.tensor_tensor(cang, cang, turns, ALU.add))
            v.tensor_scalar(cang, cang, PI_DOWN, -PI_DOWN, ALU.min, ALU.max)
            v.tensor_scalar(ang, ang, PI_DOWN, -PI_DOWN, ALU.min, ALU.max).then_inc(angle_done, 1)
            dve.wait_ge(rope_table, 1)
            d.clear()
            dve.wait_ge(first_ada_done, 1)
            d.link(v.tensor_copy(modn[:, :], yac[:, 0, 0:N_ADA1]))
            d.clear()
            with dve.Fori(0, depth, 1) as L:
                dve.wait_ge(params_in, nth(L, 32, 32))
                d.link(v.tensor_tensor(mod[:, 0:N_ADA1], modn[:, :], par[:, 0:N_ADA1], ALU.add))
                v.scalar_tensor_tensor(gs[:, 0:KD], mod[:, 8:16], 1.0, par[:, 48:56],
                                       ALU.add, ALU.mult).then_inc(mod_ready, 1)
                normalised(0, nth(L, 2, 1))
                for m in range(AHEAD):
                    dve_low(dve, L, m)
                source_low(L, 0, B_H)
                d.clear()
                with dve.Fori(0, 3, 1) as i:
                    for c in range(4):
                        dve_low(dve, L, c + AHEAD, i)
                for m in range(12, M_G):
                    dve_low(dve, L, m + AHEAD)
                for n in range(5):
                    rope(L, n)
                for s in range(UNITS + 5):
                    if s < N_G:
                        dve_low(dve, L, M_G + s + AHEAD)
                    if 1 <= s < UNITS + 1:
                        head_d1(L, s - 1)
                    if 2 <= s < UNITS + 2:
                        head_d2(L, s - 2)
                    if 11 <= s < UNITS + 3:
                        head_d3(L, s - 3)
                    if 12 <= s < UNITS + 4:
                        head_d4(L, s - 4)
                    if 5 <= s:
                        head_out(L, s - 5)
                source_low(L, 1, B_Y)
                dve.wait_ge(acc_free, nth(L, EVACS, E_WQ + 2))
                d.link(v.tensor_tensor(mod[:, N_ADA1:48], mod[:, N_ADA1:48], par[:, N_ADA1:48], ALU.add))
                d.link(v.scalar_tensor_tensor(gs[:, KD:2 * KD], mod[:, 32:40], 1.0, par[:, 56:64],
                                              ALU.add, ALU.mult))
                d.clear()
                with dve.Fori(0, N_BR // 4, 1) as i:
                    dve.wait_ge(sig_done, nth(L, 1, 1))
                    for c in range(4):
                        dve_low(dve, L, M_BR + c + AHEAD, i)
                        chunk_used(dve, L, M_BR + c, i)
                        ga = big[:, bass.ds(nth(i, 4 * T, B_GT + c * T), T)]
                        gb = big[:, bass.ds(nth(i, 4 * T, B_GT + (8 + c) * T), T)]
                        d.mark(v.tensor_tensor(ga, ga, pg[:, c % 2, 0:T], ALU.mult))
                        d.link(v.tensor_tensor(gb, gb, pg[:, c % 2, T:2 * T], ALU.mult))
                        v.tensor_tensor(big[:, bass.ds(nth(i, 4 * T, B_MG + c * T), T)], ga, gb,
                                        ALU.add).then_inc(pg_free, 1)
                    d.clear()
                source_low(L, 2, B_MG)
                with dve.Fori(0, N_OUT // 4, 1) as i:
                    for c in range(4):
                        dve_low(dve, L, M_OUT + c + AHEAD, i)
                        chunk_used(dve, L, M_OUT + c, i)
                        xc = x[:, bass.ds(nth(i, 4 * T, c * T), T)]
                        v.scalar_tensor_tensor(xc, pg[:, c % 2, 0:T], mod[:, bass.ds(nth(i, 4, 16 + c), 1)],
                                               xc, ALU.mult, ALU.add).then_inc(pg_free, 1)
                normalised(1, nth(L, 2, 2))
                source_low(L, 3, B_H)
                with dve.Fori(0, N_WQ // 4, 1) as i:
                    for c in range(4):
                        dve_low(dve, L, M_WQ + c + AHEAD, i)
                d.clear()
                with dve.Fori(0, ITERS, 1) as i:
                    dve.wait_ge(acc_free, nth(L, EVACS, E_U + 2))
                    for c in range(4):
                        dve_low(dve, L, M_U + c + AHEAD, i)
                        if c == 1:
                            subkey_topk(L, i)
                        if c == 3:
                            pair_topk(L, i)
                    d.clear()
                dve.wait_ge(ada_used, nth(L, N_ADA, 2 + N_ADA))
                v.tensor_copy(modn[:, :], yac[:, 0, 0:N_ADA1])
                best = top(K_BEST, 256).rearrange("p (u r) -> p u r", r=16)
                e3 = top(K_EXP, 256).rearrange("p (u r) -> p u r", r=16)
                v.tensor_tensor(e3, best, best[:, :, 0:1].to_broadcast([P, 16, 16]),
                                ALU.subtract).then_inc(gexp_in, 1)
                dve.wait_ge(gexp_done, nth(L, 1, 1))
                d.link(v.tensor_reduce(top(K_SUM, 16), e3, AX.X, ALU.add))
                d.link(v.reciprocal(top(K_SUM + 16, 16), top(K_SUM, 16)))
                dve.wait_ge(decode_done, nth(L, UNITS, UNITS))
                v.tensor_tensor(top(K_IDX + 512, 256).rearrange("p (u r) -> p u r", r=16), e3,
                                top(K_SUM + 16, 16).unsqueeze(2).to_broadcast([P, 16, 16]),
                                ALU.mult).then_inc(gates_ready, 1)
                dve.wait_ge(selT_done, nth(L, 1, 1))
                for t in range(TT):
                    tok = slice(t * P, (t + 1) * P)
                    v.tensor_copy(selT[:, :, tok], pg[:, t, 0:T].rearrange("p (n t) -> p n t", n=2))
                    d.mark(v.tensor_copy(selg[:, 0, tok], pg[:, t, T:384]))
                d.join()
                for t in range(TT):
                    tok = slice(t * P, (t + 1) * P)
                    ins = v.tensor_tensor(selg[:, 1, tok], pg[:, t, T:384], selg[:, 0, tok].bitcast(F32), ALU.subtract)
                ins.then_inc(sel_ready, 1)
                dve.wait_ge(sel_ready, nth(L, 1, 1))
                mask(L, 0, 0, 0)
                d.mark(mask_times(0, 1, 0))
                mask_times(0, 0, 0).then_inc(ohj_done, 1)
                d.clear()

                chunks_and_gates(L, M_U + HALF, 0, 0, first=True)
                d.clear()
                with dve.Fori(1, ITERS - 1, 1) as i:
                    chunks_and_gates(L, M_U + HALF, 0, i)
                    d.clear()
                chunks_and_gates(L, M_U + HALF, 0, ITERS - 1, last=True)
                gate(L, 0, 1, ITERS - 1)
                a_low(L, 0, 0, 0)
                d.clear()
                chunks_and_gates(L, M_VV, 1, 0, first=True, values=True)
                d.clear()
                with dve.Fori(1, ITERS - 1, 1) as i:
                    chunks_and_gates(L, M_VV, 1, i, values=True)
                    d.clear()
                chunks_and_gates(L, M_VV, 1, ITERS - 1, last=True, values=True)
                gate(L, 1, 1, ITERS - 1)
                a_low(L, 1, 0, 0)
                with dve.Fori(0, ITERS - 1, 1) as i:
                    for q in range(2):
                        a_low(L, 1, q + 1, i)
                        for c in (2 * q, 2 * q + 1):
                            dve_low(dve, L, M_VV + HALF + c + AHEAD, i)
                a_low(L, 1, 1, ITERS - 1)
                dve_low(dve, L, M_VV + HALF + AHEAD, ITERS - 1)
                chunk_used(dve, L, SPLITS - 1)
                for t in range(TT):
                    ins = v.tensor_copy(col(t * D, D), yac[:, 2 * t:2 * t + 2, :])
                ins.then_inc(ytok_taken, 1)
                for g in range(4):
                    out = acc[:, g, :] if g < 2 else pg[:, g - 2, :]
                    dve.wait_ge(yT_done, nth(L, 4, g + 1))
                    for k in (2 * g, 2 * g + 1):
                        xc = x[:, k * T:(k + 1) * T]
                        ins = v.scalar_tensor_tensor(xc, out[:, k % 2 * T:(k % 2 + 1) * T],
                                                     mod[:, 40 + k:41 + k], xc, ALU.mult, ALU.add)
                    ins.then_inc(xT_taken, 1)
                d.clear()
            normalised(2, 2 * depth + 1)

        @block.gpsimd
        def _(pool):
            g = nc.gpsimd
            s = Steps(pool, pool_step)
            with pool.Fori(0, depth, 1) as L:
                with pool.Fori(0, UNITS, 1) as i:
                    pool.wait_ge(topk_done, nth(L, UNITS, 1, i, 1))
                    rec = top(K_PREC, 64)
                    s.link(g.tensor_copy(rec, big[:, bass.ds(nth(i, 64, B_TK + K_RECS), 64)]))
                    eq = top(K_PEQ, 256).rearrange("p (r a) -> p r a", a=16)
                    shape = [P, 16, 16]
                    for p in range(2):
                        s.link(g.tensor_tensor(eq, rec[:, 32 + 16 * p:48 + 16 * p].unsqueeze(2).to_broadcast(shape),
                                               iota16.unsqueeze(1).to_broadcast(shape), ALU.subtract))
                        s.link(g.tensor_scalar(eq, eq, 0.0, None, ALU.is_equal))
                        s.link(g.tensor_tensor(eq, eq, rec[:, 16 * p:16 * p + 16].unsqueeze(1).to_broadcast(shape),
                                               ALU.mult))
                        for n in (8, 4, 2):
                            s.link(g.tensor_tensor(eq[:, :, 0:n], eq[:, :, 0:n], eq[:, :, n:2 * n], ALU.add))
                        s.link(g.tensor_tensor(top(K_PRES + 16 * p, 16).unsqueeze(2), eq[:, :, 0:1], eq[:, :, 1:2],
                                               ALU.add))
                    dst = top(K_IDX, 512).rearrange("p (n c) -> p n c", n=2)[:, :, bass.ds(i * 16, 16)]
                    g.tensor_copy(dst, top(K_PRES, 32).rearrange("p (n c) -> p n c", n=2)).then_inc(decode_done, 1)
                    s.clear()
                for half in range(2):
                    with pool.Fori(0, NG // 2, 1) as i:
                        pool.wait_ge(sel_ready, nth(L, 1, 1))
                        for q in range(4):
                            pool.wait_ge(g_done, nth(L, 4 * NG, 2 * half * NG + q + 1, i, 4))
                            s.link(g.tensor_copy(selc[:, q % 2, :],
                                                 selT[:, 0, bass.ds(nth(i, 4 * GS, q * GS), GS)]))
                            for t in range(GS):
                                ins = g.tensor_scalar(ohi[:, q % 2, t, :], iota, selc[:, q % 2, t:t + 1], None,
                                                      ALU.is_equal)
                            ins.then_inc(ohi_done, 1)
                        s.clear()


def to_stream(w):
    depth, rows, cols = w.shape
    assert rows == D
    return w.reshape(depth, KD, P, cols // P, P).transpose(0, 3, 2, 1, 4).reshape(depth, cols // P, P, CH)


def kernel(x, c, positions, ada_w, ada_b, norm1_g, w_in, swa_sinks, w_branch_swa, w_branch_sb,
           w_out, norm2_g, peer_wq, peer_subkeys, peer_u, peer_v, final_g):
    import concourse.bacc as bacc
    from concourse.bass_utils import run_bass_kernel_spmd as run

    arr = np.asarray
    x, c, positions = arr(x), arr(c), arr(positions)
    w_in, ada_w, ada_b = arr(w_in), arr(ada_w), arr(ada_b)
    depth = w_in.shape[0]
    f32 = np.float32

    heads = np.arange(8).reshape(2, 4).T.ravel()
    swa_cols = (heads[:, None] * HD + np.arange(HD)[None, :]).ravel()
    off = np.cumsum([0, 512, 128, 128, 512, 512, 512, 1024, 1024])
    qa, ka, va, qb, kb, vb, ga, gb = [np.arange(off[n], off[n + 1]) for n in range(8)]
    order = np.concatenate([qa[swa_cols], qb, kb, ka, va, vb])
    gates = np.concatenate([ga, gb])

    def columns(v, n):
        return arr(v).reshape(depth, n, P).transpose(0, 2, 1)

    params = np.zeros((depth, P, 72), f32)
    params[:, :, 0:48] = columns(ada_b, 48)
    params[:, :, 48:56] = columns(norm1_g, KD)
    params[:, :, 56:64] = columns(norm2_g, KD)
    params[:, :, 64:72] = arr(swa_sinks)[:, None, :]
    sub = arr(peer_subkeys).reshape(depth, 2, 8, P, P).transpose(0, 1, 4, 2, 3)
    sub = np.ascontiguousarray(sub.reshape(depth, 2, P, CH).transpose(0, 2, 1, 3)).reshape(depth, P, 2 * CH)
    ada = np.zeros((depth * N_ADA + N_ADA1, P, CH), f32)
    ada[:depth * N_ADA] = to_stream(ada_w).reshape(-1, P, CH)
    whole = np.zeros((depth * SPLITS + RAW, P, CH), f32)
    stream = whole[:depth * SPLITS].reshape(depth, SPLITS, P, CH)
    branch = np.concatenate([arr(w_branch_swa)[:, swa_cols], arr(w_branch_sb)], 1)
    for m, w in ((M_QK, w_in[:, :, order]), (M_G, w_in[:, :, gates]), (M_BR, branch),
                 (M_OUT, arr(w_out)), (M_WQ, arr(peer_wq))):
        s = to_stream(w)
        stream[:, m:m + s.shape[1]] = s
    u = arr(peer_u).reshape(depth, P, P, KD, P)
    stream[:, M_U:M_VV] = u.transpose(0, 2, 4, 3, 1).reshape(depth, N_U, P, CH)
    stream[:, M_VV:] = arr(peer_v).reshape(depth, P, P, D).transpose(0, 2, 1, 3)

    arrays = {
        "consts": constants(),
        "stream": whole,
        "ada": ada,
        "subkeys": sub,
        "params": params,
        "xT": np.ascontiguousarray(x[0].reshape(T, KD, P).transpose(2, 1, 0).reshape(P, KD * T)),
        "cT": np.ascontiguousarray(c[0].reshape(KD, P).T),
        "pos": np.ascontiguousarray(np.broadcast_to(positions, (P, T))).astype(np.int32),
        "final_g": np.ascontiguousarray(arr(final_g).reshape(KD, P).T),
    }
    nc = bacc.Bacc("TRN2", target_bir_lowering=False, num_devices=1, dynamic_dma_scratch_size=64)
    aps = [nc.dram_tensor(k, v.shape, mybir.dt.from_np(v.dtype), kind="ExternalInput").ap()
           for k, v in arrays.items()]
    out = nc.dram_tensor("outT", (P, KD * T), F32, kind="ExternalOutput").ap()
    build(nc, depth, *aps, out)
    got = run(nc, [arrays], core_ids=[0]).results[0]["outT"]
    return got.reshape(P, KD, T).transpose(2, 1, 0).reshape(1, T, D)
```

```python
from contextlib import ExitStack

import numpy as np

import concourse.bass as bass
from concourse import mybir

F32 = mybir.dt.float32
F32R = mybir.dt.float32r
BF16 = mybir.dt.bfloat16
I32 = mybir.dt.int32
U32 = mybir.dt.uint32
ACT = mybir.ActivationFunctionType
ALU = mybir.AluOpType
AX = mybir.AxisListType

P = 128
D = 1024
KD = D // P
T = 256
TT = T // P
HD = 64
CH = KD * P
RAW = 4
W = 4
AHEAD = 3
POOL_LOW = 2

N_QA, N_V, N_PAD, N_QB, N_G, N_BR, N_OUT, N_WQ, N_U, N_VV = 5, 5, 2, 8, 16, 8, 8, 16, 128, 128
SPLITS = N_QA + N_V + N_PAD + N_QB + N_G + N_BR + N_OUT + N_WQ + N_U + N_VV
N_ADA, N_ADA1 = 48, 16
N_ADA2 = N_ADA - N_ADA1
SA = 4
M_QA = 0
M_V = M_QA + N_QA
M_PAD = M_V + N_V
M_QB = M_PAD + N_PAD
M_G = M_QB + N_QB
M_BR = M_G + N_G
M_OUT = M_BR + N_BR
M_WQ = M_OUT + N_OUT
M_U = M_WQ + N_WQ
M_VV = M_U + N_U
assert SPLITS % RAW == 0 and M_G % W == 0 and M_U % W == 0

E_QA = 0
E_V = E_QA + N_QA
E_QB = E_V + N_V
E_WQ = E_QB + N_QB + N_G
E_SK = E_WQ + N_WQ
E_U = E_SK + 8
EVACS = E_U + N_U // 2
assert EVACS % 2 == 0

HALF = 64
GT = 8
GS = GT // 2
GP = 3
NG = T // GT
ITERS = HALF // 4
LAST_HEAD = [5, 6, 7, 8, 10, 12, 14, 16]
UNITS = 16

C_ID, C_TRI, C_ROT = 0, 128, 256
C_SWB = 384
C_SBM = C_SWB + 384
C_ONE = C_SBM + P
C_IOTA = C_SBM + T
C_MISC = C_IOTA + 128
NCONST = C_MISC + 4

B_QK = 0
B_VT = B_QK + 13 * T
B_GT = B_VT + TT * 640
B_Y = B_GT + 16 * T
B_MG = B_Y + KD * T
B_AT = B_MG + KD * T
RU = 8
B_SQ = B_GT
B_ADA0 = B_SQ + 8 * T
B_H = B_Y
HB = HALF * T
B_QP = HB
B_SKV = B_QP + 16 * T
B_TK = B_SKV + 16 * 256
B_SUB = 2 * HB - 16 * P
B_RMS = B_SUB - T
B_ADA = B_RMS - SA * CH
B_RES = B_ADA - 2 * 2 * P
K_CUR, K_CUT, K_VAL, K_CAND, K_CCUT, K_REC, K_BEST8, K_POS = 0, 256, 512, 544, 800, 1056, 1120, 1136
K_BEST = 1152
K_RECS = K_BEST + 256
K_IDX = K_RECS + 16 * 64
K_PEQ = K_IDX + 768
K_PRES = K_PEQ + 256
K_EXP = K_PRES + 32
K_SUM = K_EXP + 256
assert B_MG + 14 * CH <= B_RES and B_ADA0 + 2 * CH <= B_Y
assert B_AT + RU * 4 * 384 <= B_RES and B_TK + K_SUM + 32 <= B_RMS

NEG = -1e30
LOWEST = -3.0e38
TWO_PI_1 = 6.28125
TWO_PI_2 = float(np.float32(2 * np.pi - TWO_PI_1) // 2 ** -19 * 2 ** -19)
TWO_PI_3 = float(2 * np.pi - TWO_PI_1 - TWO_PI_2)
PI_DOWN = 3.1415925
ROUND = 12582912.0


def constants():
    c = np.zeros((P, NCONST), np.float32)
    a = np.arange(P)
    c[:, C_ID:C_ID + P] = np.eye(P)
    c[:, C_TRI:C_TRI + P] = a[:, None] >= a[None, :]
    for d in range(P):
        lo = d % HD < HD // 2
        c[d + HD // 2 if lo else d - HD // 2, C_ROT + d] = -1.0 if lo else 1.0
    q, k = a[:, None], a[None, :]
    c[:, C_SWB:C_SWB + P] = np.where(k <= q, 0.0, NEG)
    diff = q + P - np.arange(T)[None, :]
    c[:, C_SWB + P:C_SWB + P + T] = np.where((diff >= 0) & (diff < 128), 0.0, NEG)
    c[:, C_SBM:C_SBM + T] = a[:, None] < np.arange(T)[None, :]
    c[:, C_IOTA:C_IOTA + P] = a[None, :]
    half = HD // 2
    inv = np.power(np.float32(10000.0), -np.arange(half, dtype=np.float32) * np.float32(2.0 / HD))
    c[:, C_MISC] = inv[a % half]
    c[:, C_MISC + 1] = 1e-6
    c[:, C_MISC + 2] = 1.0
    return c



def build(nc, depth, consts, stream, ada, subkeys, params, xT, cT, pos, final_g, outT):
    with ExitStack() as ctx:
        def sb(name, shape, dt=F32):
            return ctx.enter_context(nc.sbuf_tensor(name, shape, dt))

        def sem(name):
            return ctx.enter_context(nc.semaphore(name))

        big = sb("big", [P, 2 * HB])
        raw = sb("raw", [P, RAW, CH])
        wsp = sb("wsp", [P, W, 2, CH], F32R)
        hs = sb("hs", [P, 2, KD * T], F32R)
        x = sb("x", [P, KD * T])
        con = sb("con", [P, NCONST])
        cosT = sb("cosT", [P, T])
        sinT = sb("sinT", [P, T])
        selT = sb("selT", [P, 2, T], BF16)
        selg = sb("selg", [P, GP, T], BF16)
        iota8 = sb("iota8", [P, P, GT], BF16)
        ohi = sb("ohi", [P, 2, P, GT], BF16)
        eqj = sb("eqj", [P, HALF, GT], BF16)
        ohj = sb("ohj", [P, 2, GP, HALF, GT], BF16)
        cact = sb("cact", [P, 2 * KD])
        par = sb("par", [P, 72])
        mod = sb("mod", [P, 48])
        modn = sb("modn", [P, N_ADA1])
        gs = sb("gs", [P, 2 * KD])
        fg = sb("fg", [P, KD])
        st = sb("st", [P, 4, 16])

        acc = ctx.enter_context(nc.psum_tensor("acc", [P, 2, 512], F32))
        pg = ctx.enter_context(nc.psum_tensor("pg", [P, 2, 512], F32))
        yac = ctx.enter_context(nc.psum_tensor("yac", [P, 4, 512], F32))

        inputs_in = sem("inputs_in")
        landed = [sem(f"landed{s}") for s in range(RAW)]
        params_in = sem("params_in")
        subkeys_in = sem("subkeys_in")
        first_ada_in = [sem(f"first_ada_in{n}") for n in range(4)]
        first_ada_sums = sem("first_ada_sums")
        first_ada_done = sem("first_ada_done")
        ada_in = [sem(f"ada_in{g}") for g in range(SA)]
        ada_ready = sem("ada_ready")
        vT_done = sem("vT_done")
        vtok_ready = sem("vtok_ready")
        ada_used = sem("ada_used")
        hi_done = sem("hi_done")
        split_done = sem("split_done")
        chunk_done = sem("chunk_done")
        acc_free = sem("acc_free")
        pg_free = sem("pg_free")
        pool_low_done = sem("pool_low_done")
        cact_ready = sem("cact_ready")
        angle_done = sem("angle_done")
        rope_table = sem("rope_table")
        mod_ready = sem("mod_ready")
        sq_done = sem("sq_done")
        ssq_done = sem("ssq_done")
        rms_done = sem("rms_done")
        xn_done = sem("xn_done")
        src_hi = sem("src_hi")
        src_done = sem("src_done")
        rot_done = sem("rot_done")
        rope_done = sem("rope_done")
        sc_done = sem("sc_done")
        d1_done = sem("d1_done")
        a1_done = sem("a1_done")
        d2_done = sem("d2_done")
        b_done = sem("b_done")
        d3_done = sem("d3_done")
        a2_done = sem("a2_done")
        d4_done = sem("d4_done")
        av_done = sem("av_done")
        y_taken = sem("y_taken")
        sig_done = sem("sig_done")
        sk_done = sem("sk_done")
        topk_done = sem("topk_done")
        decode_done = sem("decode_done")
        gexp_in = sem("gexp_in")
        gexp_done = sem("gexp_done")
        gates_ready = sem("gates_ready")
        selT_done = sem("selT_done")
        oh_done = sem("oh_done")
        g_done = sem("g_done")
        mul_done = sem("mul_done")
        ahi_done = sem("ahi_done")
        alo_done = sem("alo_done")
        ytok_taken = sem("ytok_taken")
        yT_done = sem("yT_done")
        xT_taken = sem("xT_taken")
        out_stored = sem("out_stored")
        dve_step = sem("dve_step")
        act_step = sem("act_step")
        pool_step = sem("pool_step")

        def col(base, n=1):
            return big[:, base:base + n]

        ident = con[:, C_ID:C_ID + P]
        tri = con[:, C_TRI:C_TRI + P]
        ones = con[:, C_ONE:C_ONE + P]
        rot = con[:, C_ROT:C_ROT + P]
        iota = con[:, C_IOTA:C_IOTA + P]
        iota16 = con[:, C_IOTA:C_IOTA + 16]
        invf = con[:, C_MISC:C_MISC + 1]
        eps = con[:, C_MISC + 1:C_MISC + 2]
        one = con[:, C_MISC + 2:C_MISC + 3]
        rms = col(B_RMS, T)
        sinks = par[:, 64:72]

        def adab(g, n=CH):
            return col(B_ADA + g * CH, n)

        def ada_first(a):
            return col(B_MG + a * CH if a < 14 else B_ADA0 + (a - 14) * CH, CH)

        def qk(c):
            return col(B_QK + c * T, T)

        def vtok(t):
            return col(B_VT + t * 640, 640)

        def att(u, b):
            return col(B_AT + ((u % RU) * 4 + b) * 384, 384)

        def top(base, n):
            return col(B_TK + base, n)

        def half_of(h):
            return big[:, h * HB:(h + 1) * HB]

        class Steps:

            def __init__(self, eng, s):
                self.eng, self.s, self.n = eng, s, 0

            def mark(self, ins):
                self.n += 1
                ins.then_inc(self.s, 1)

            def join(self):
                self.eng.wait_ge(self.s, self.n)

            def link(self, ins):
                self.mark(ins)
                self.join()

            def clear(self):
                if self.n:
                    self.join()
                    self.eng.sem_clear(self.s)
                    self.n = 0

        def nth(L, per_layer, k, i=0, per=0):
            return L * per_layer + i * per + k

        def raw_landed(eng, L, n, i=0):
            eng.wait_ge(landed[n % RAW], nth(L, SPLITS // RAW * 16, (n // RAW + 1) * 16, i, 16))

        def act_high(act, L, m, i=0):
            raw_landed(act, L, m, i)
            act.wait_ge(chunk_done, nth(L, SPLITS, m + 1, i, 4))
            n = P if M_PAD <= m < M_QB and isinstance(i, int) else CH
            nc.scalar.activation(wsp[:, m % W, 0, 0:n], raw[:, m % RAW, 0:n],
                                 ACT.Copy).then_inc(hi_done, 1)

        def dve_low(dve, L, m, i=0):
            dve.wait_ge(hi_done, nth(L, SPLITS, m + 1, i, 4))
            n = P if M_PAD <= m < M_QB and isinstance(i, int) else CH
            nc.vector.tensor_tensor(wsp[:, m % W, 1, 0:n], raw[:, m % RAW, 0:n],
                                    wsp[:, m % W, 0, 0:n].bitcast(F32),
                                    ALU.subtract).then_inc(split_done, 1)

        def chunk_split(pe, L, m, i=0):
            pe.wait_ge(split_done, nth(L, SPLITS, m + 1, i, 4))

        def chunk_used(eng, L, m, i=0):
            eng.wait_ge(chunk_done, nth(L, SPLITS, W + m + 1, i, 4))

        TERMS = ((0, 1), (1, 0), (0, 0))

        def product(pe, out, m, k0=0, k1=KD, L=None, source=None):
            mm = None
            for k in range(k0, k1):
                if source is not None:
                    pe.wait_ge(src_done, nth(L, 4 * KD, source * KD + k + 1))
                for n, (a, b) in enumerate(TERMS):
                    mm = pe.matmul(out, wsp[:, m % W, a, k * P:(k + 1) * P], hs[:, b, k * T:(k + 1) * T],
                                   start=(k == k0 and n == 0), stop=(k == k1 - 1 and n == 2))
            return mm

        block = ctx.enter_context(nc.Block())

        @block.sync
        def _(sp):
            sp.dma_start(con[:, :], consts).then_inc(inputs_in, 16)
            sp.dma_start(x[:, :], xT).then_inc(inputs_in, 16)
            sp.dma_start(cact[:, 0:KD], cT).then_inc(inputs_in, 16)
            sp.dma_start(cosT[:, :].bitcast(I32), pos).then_inc(inputs_in, 16)
            sp.dma_start(fg[:, :], final_g).then_inc(inputs_in, 16)

            def load(n, L, i, per):
                src = stream[bass.ds(nth(L, SPLITS, n, i, per), 1), :, :]
                sp.dma_start(raw[:, n % RAW, :], src.rearrange("a p c -> p (a c)")).then_inc(landed[n % RAW], 16)

            def load_ada(L, a, i=0, per=0):
                sp.wait_ge(ada_ready, nth(L, N_ADA, a + 1, i, per))
                src = ada[bass.ds(nth(L, N_ADA, N_ADA1 + a, i, per), 1), :, :]
                sp.dma_start(adab(a % SA), src.rearrange("a p c -> p (a c)")).then_inc(ada_in[a % SA], 16)

            def load_next(L, n, i=0, per=4):
                sp.wait_ge(split_done, nth(L, SPLITS, n - RAW + 1, i, per))
                load(n, L, i, per)

            for a in range(N_ADA1):
                sp.dma_start(ada_first(a), ada[a, :, :]).then_inc(first_ada_in[a // 4], 16)
                if a % 4 == 3:
                    sp.dma_start(raw[:, a // 4, :], stream[a // 4, :, :]).then_inc(landed[a // 4], 16)
            with sp.Fori(0, depth, 1) as L:
                sp.wait_ge(ytok_taken, nth(L, 2, 2))
                sp.dma_start(par[:, :], params[bass.ds(L, 1), :, :].rearrange("a p c -> p (a c)")).then_inc(
                    params_in, 16)
                for a in range(SA):
                    load_ada(L, a)
                sp.dma_start(col(B_SUB, 2 * CH), subkeys[bass.ds(L, 1), :, :].rearrange("a p c -> p (a c)")).then_inc(
                    subkeys_in, 16)
                with sp.Fori(0, (N_ADA2 - SA) // 4, 1) as i:
                    for c in range(4):
                        load_next(L, RAW + c, i)
                        load_ada(L, SA + c, i, 4)
                for c in range(SA):
                    load_next(L, RAW + N_ADA2 - SA + c)
                with sp.Fori(0, N_ADA1 // 4, 1) as i:
                    for c in range(8):
                        load_next(L, RAW + N_ADA2 + c, i, 8)
                        if c % 2 == 0:
                            load_ada(L, N_ADA2 + c // 2, i, 4)
                done = N_ADA2 + 2 * N_ADA1
                with sp.Fori(0, (SPLITS - done) // 4, 1) as i:
                    for c in range(4):
                        load_next(L, RAW + done + c, i)
            sp.wait_ge(xn_done, (2 * depth + 1) * KD)
            sp.dma_start(outT, col(B_H, KD * T)).then_inc(out_stored, 16)
            sp.wait_ge(out_stored, 16)

        @block.tensor
        def _(pe):
            pe.sem_inc(chunk_done, W)
            pe.sem_inc(ada_used, 2)
            pe.sem_inc(g_done, 2)

            def ssq(norm):
                for k in range(KD):
                    pe.wait_ge(sq_done, (norm - 1) * KD + k + 1)
                    mm = pe.matmul(yac[:, 1, 0:T], ones, col(B_SQ + k * T, T),
                                   start=(k == 0), stop=(k == KD - 1))
                mm.then_inc(ssq_done, 1)

            def ada_whole(out, w):
                for k in range(KD):
                    mm = pe.matmul(out, w[:, k * P:(k + 1) * P], cact[:, KD + k:KD + k + 1],
                                   start=(k == 0), stop=(k == KD - 1), skip_group_check=True)
                return mm

            def ada_sums(out, w):
                pe.matmul(out, w[:, 0:P], ones[:, 0:1], start=True, stop=False, skip_group_check=True)
                return pe.matmul(out, w[:, P:2 * P], ones[:, 0:1], start=False, stop=True, skip_group_check=True)

            def ada_product(L, a, out, i=0, per=0):
                pe.wait_ge(ada_ready, nth(L, N_ADA, SA + a + 1, i, per))
                ada_sums(out, col(B_RES + a % 2 * 2 * P, 2 * P)).then_inc(ada_used, 1)

            def ada_beside(L, e, i=0):
                if e < N_ADA2:
                    ada_product(L, e, acc[:, e % 2, T:T + 1], i, 4)

            def by_features(L, m, e, i=0, source=None):
                pe.wait_ge(acc_free, nth(L, EVACS, e + 1, i, 4))
                ada_beside(L, e, i)
                chunk_split(pe, L, m, i)
                product(pe, acc[:, e % 2, 0:T], m, L=L, source=source).then_inc(chunk_done, 1)

            def rotate(L, n):
                c = n if n < 4 else 12
                e = E_QA + n
                pe.wait_ge(acc_free, nth(L, EVACS, e + 3))
                out = pg[:, n // 2, n % 2 * T:(n % 2 + 1) * T] if n < 4 else yac[:, 0, 0:T]
                pe.matmul(out, rot, qk(c), start=True, stop=True).then_inc(rot_done, 1)

            def v_transposed(L, c):
                pe.wait_ge(acc_free, nth(L, EVACS, E_V + c + 3))
                for t in range(TT):
                    mm = pe.transpose(yac[:, 1 + c // 2, c % 2 * T + t * P:c % 2 * T + (t + 1) * P],
                                      att(c, 1)[:, t * P:(t + 1) * P], ident)
                mm.then_inc(vT_done, 1)

            def head_scores(L, u):
                out = pg[:, u % 2, :]
                if u < 2:
                    pe.wait_ge(rope_done, nth(L, 5, 5))
                if u >= 2:
                    pe.wait_ge(d1_done, nth(L, UNITS, u - 1))
                if u < 8:
                    b, q, k = HD * (u // 4), qk(u % 4), qk(12)
                    pe.matmul(out[:, 0:P], q[b:b + HD, 0:P], k[b:b + HD, 0:P], start=True, stop=True)
                    mm = pe.matmul(out[:, P:384], q[b:b + HD, P:T], k[b:b + HD, 0:T], start=True, stop=True)
                else:
                    h = u - 8
                    b, q, k = HD * (h % 2), qk(4 + h // 2), qk(8 + h // 2)
                    pe.wait_ge(acc_free, nth(L, EVACS, E_QB + h // 2 * 2 + 1 + 3))
                    pe.matmul(out[:, 0:T], k[b:b + HD, 0:P], q[b:b + HD, 0:T], start=True, stop=True)
                    mm = pe.matmul(out[:, T:384], k[b:b + HD, P:T], q[b:b + HD, P:T], start=True, stop=True)
                mm.then_inc(sc_done, 1)

            def head_middle(L, u):
                out = yac[:, u % 2, :]
                pe.wait_ge(d2_done, nth(L, UNITS, u + 1))
                if u == 0:
                    pe.wait_ge(vtok_ready, nth(L, 3, 3))
                if 2 <= u < 10:
                    pe.wait_ge(a2_done, nth(L, UNITS, u - 1))
                elif u >= 10:
                    pe.wait_ge(d3_done, nth(L, 8, u - 9))
                if u < 8:
                    for j in range(3):
                        mm = pe.transpose(out[:, j * P:(j + 1) * P], att(u, 1)[:, j * P:(j + 1) * P], ident)
                else:
                    s = att(u, 3)
                    pe.matmul(out[:, 0:T], tri, s[:, 0:T], start=True, stop=False, skip_group_check=True)
                    pe.matmul(out[:, P:T], ones, s[:, T:384], start=False, stop=True, skip_group_check=True)
                    mm = pe.matmul(out[:, T:384], tri, s[:, T:384], start=True, stop=True, skip_group_check=True)
                mm.then_inc(b_done, 1)

            def head_values(L, u):
                if u < 8:
                    pe.wait_ge(a2_done, nth(L, UNITS, u + 1))
                    b, vc = HD * (u // 4), HD * (u // 4)
                else:
                    h = u - 8
                    pe.wait_ge(d4_done, nth(L, 8, h + 1))
                    b, vc = HD * (h % 2), P + HD * h
                w = att(u, 2)
                if u >= 2:
                    pe.wait_ge(y_taken, nth(L, UNITS, u - 1))
                out = yac[b:b + HD, 2 + u % 2, :]
                pe.matmul(out[:, 0:T], vtok(0)[:, vc:vc + HD], w[:, 0:T], start=True, stop=False,
                          skip_group_check=True)
                pe.matmul(out[:, P:T], vtok(1)[:, vc:vc + HD], w[:, T:384], start=False, stop=True,
                          skip_group_check=True).then_inc(av_done, 1)

            def gate_matrices(L, half, s, i):
                g, b = s // 2 % 2, s % 2
                if b == 0:
                    k = half * NG + s // 2
                    pe.wait_ge(oh_done, nth(L, 2 * NG, k + 1, i, 2))
                    pe.wait_ge(mul_done, nth(L, 2 * NG, k + 1, i, 2))
                for t in range(b * GS, (b + 1) * GS):
                    for a in range(GP - 1, -1, -1):
                        mm = pe.matmul(pg[:, g, t * HALF:(t + 1) * HALF], ohi[:, g, :, t],
                                       ohj[:, g, a, :, t], start=(a == GP - 1), stop=(a == 0))
                mm.then_inc(g_done, 1)

            def expert_pair(L, half, c, i, gates=False):
                m = M_U + half * HALF + c
                e = E_U + (half * HALF + c) // 2
                for a in range(2):
                    if a == 0:
                        pe.wait_ge(acc_free, nth(L, EVACS, e + 1, i, 2))
                    chunk_split(pe, L, m + a, i)
                    product(pe, acc[:, e % 2, a * T:(a + 1) * T], m + a).then_inc(chunk_done, 1)
                    if gates:
                        gate_matrices(L, 0, c + a - 4, i)

            def value_chunk(L, half, c, i, start=False, stop=False):
                m = M_VV + half * HALF + c
                if c % 2 == 0:
                    pe.wait_ge(alo_done, nth(L, HALF, (half * HALF + c) // 2 + 1, i, 2))
                chunk_split(pe, L, m, i)
                for t in range(TT):
                    for n, (a, b) in enumerate(TERMS):
                        for w in range(2):
                            mm = pe.matmul(yac[:, 2 * t + w, :], hs[:, b, c * T + t * P:c * T + (t + 1) * P],
                                           wsp[:, m % W, a, w * 512:(w + 1) * 512],
                                           start=(start and n == 0), stop=(stop and n == 2),
                                           skip_group_check=True)
                mm.then_inc(chunk_done, 1)

            pe.wait_ge(inputs_in, 80)
            pe.wait_ge(cact_ready, 1)
            for a in range(N_ADA1):
                if a % 2 == 0:
                    pe.wait_ge(first_ada_in[a // 4], 64)
                    mm = ada_whole(yac[:, 0, a:a + 1], ada_first(a))
                else:
                    pe.wait_ge(first_ada_sums, a // 2 + 1)
                    mm = ada_sums(yac[:, 0, a:a + 1], ada_first(a))
            mm.then_inc(first_ada_done, 1)
            with pe.Fori(0, depth, 1) as L:
                ssq(nth(L, 2, 1))
                for c in range(N_QA):
                    by_features(L, M_QA + c, E_QA + c, source=None if c else 0)
                for c in range(N_V):
                    by_features(L, M_V + c, E_V + c)
                for m in range(M_PAD, M_QB):
                    chunk_split(pe, L, m)
                    pe.matmul(yac[:, 2, 0:2], wsp[:, m % W, 0, 0:P], wsp[:, m % W, 1, 0:2],
                              start=True, stop=True).then_inc(chunk_done, 1)
                for n in range(5):
                    rotate(L, n)
                for c in range(N_V):
                    v_transposed(L, c)
                for s in range(N_QB + N_G):
                    by_features(L, M_QB + s, E_QB + s)
                    if s < UNITS:
                        head_scores(L, s)
                    if 2 <= s < UNITS + 2:
                        head_middle(L, s - 2)
                    if 4 <= s < UNITS + 4:
                        head_values(L, s - 4)

                def ada_next(L, a, c, i):
                    if c % 2:
                        ada_product(L, N_ADA2 + a + c // 2, yac[:, 0, bass.ds(nth(i, 2, a + c // 2), 1)], i, 2)

                with pe.Fori(0, N_BR // 4, 1) as i:
                    for c in range(4):
                        chunk_split(pe, L, M_BR + c, i)
                        pe.wait_ge(pg_free, nth(L, N_BR + N_OUT, c + 1, i, 4))
                        first = None if c else 1
                        product(pe, pg[:, c % 2, 0:T], M_BR + c, 0, 4, L, first)
                        product(pe, pg[:, c % 2, T:2 * T], M_BR + c, 4, 8, L, first).then_inc(chunk_done, 1)
                        ada_next(L, 0, c, i)
                with pe.Fori(0, N_OUT // 4, 1) as i:
                    for c in range(4):
                        chunk_split(pe, L, M_OUT + c, i)
                        pe.wait_ge(pg_free, nth(L, N_BR + N_OUT, N_BR + c + 1, i, 4))
                        product(pe, pg[:, c % 2, 0:T], M_OUT + c, L=L,
                                source=None if c else 2).then_inc(chunk_done, 1)
                        ada_next(L, 4, c, i)
                ssq(nth(L, 2, 2))
                with pe.Fori(0, N_WQ // 4, 1) as i:
                    for c in range(4):
                        by_features(L, M_WQ + c, E_WQ + c, i, source=None if c else 3)
                        ada_next(L, 8, c, i)
                pe.wait_ge(subkeys_in, nth(L, 16, 16))
                for e in range(8):
                    t, q = e // 4, e % 4
                    pe.wait_ge(acc_free, nth(L, EVACS, E_SK + e + 1 if e > 1 else E_SK + 2))
                    for n in range(4):
                        mm = pe.matmul(acc[:, e % 2, n * P:(n + 1) * P],
                                       col(B_QP + (4 * q + n) * T + t * P, P),
                                       col(B_SUB + (4 * q + n) * P, P), start=True, stop=True)
                    mm.then_inc(sk_done, 1)
                with pe.Fori(0, ITERS, 1) as i:
                    expert_pair(L, 0, 0, i)
                    expert_pair(L, 0, 2, i)
                for c in (0, 2):
                    expert_pair(L, 1, c, 0)
                pe.wait_ge(gates_ready, nth(L, 1, 1))
                for t in range(TT):
                    for n in range(3):
                        mm = pe.transpose(pg[:, t, n * P:(n + 1) * P], top(K_IDX + n * T + t * P, P), ident)
                mm.then_inc(selT_done, 1)
                with pe.Fori(1, ITERS, 1) as i:
                    for g in range(2):
                        expert_pair(L, 1, 2 * g, i, gates=True)
                for c in range(4):
                    gate_matrices(L, 0, c, ITERS - 1)

                def values_and_gates(i, start=False):
                    for c in range(4):
                        gate_matrices(L, 1, c, i)
                        value_chunk(L, 0, c, i, start=start and c == 0)

                values_and_gates(0, start=True)
                with pe.Fori(1, ITERS, 1) as i:
                    values_and_gates(i)
                with pe.Fori(0, ITERS - 1, 1) as i:
                    for c in range(4):
                        value_chunk(L, 1, c, i)
                for c in range(4):
                    value_chunk(L, 1, c, ITERS - 1, stop=(c == 3))
                pe.wait_ge(ytok_taken, nth(L, 2, 4))
                for g in range(4):
                    out = acc[:, g, :] if g < 2 else pg[:, g - 2, :]
                    for k in range(2):
                        for t in range(TT):
                            mm = pe.transpose(out[:, k * T + t * P:k * T + (t + 1) * P],
                                              col(t * D + (2 * g + k) * P, P), ident)
                    mm.then_inc(yT_done, 1)
            ssq(2 * depth + 1)

        @block.scalar
        def _(act):
            a = Steps(act, act_step)
            act.sem_inc(acc_free, 2)
            nc_act = nc.scalar

            def squares(k0, k1):
                for k in range(k0, k1):
                    nc_act.activation(col(B_SQ + k * T, T), x[:, k * T:(k + 1) * T], ACT.Square).then_inc(sq_done, 1)

            def root(norm):
                act.preload_act_table(ACT.Sqrt)
                act.wait_ge(ssq_done, norm)
                nc_act.activation(rms, yac[:, 1, 0:T], ACT.Sqrt, bias=eps, scale=1.0 / D).then_inc(rms_done, 1)

            def modulated(L, w):
                for k in range(KD):
                    act.wait_ge(xn_done, nth(L, 2 * KD, w * KD + k + 1))
                    nc_act.activation(hs[:, 0, k * T:(k + 1) * T], col(B_H + k * T, T), ACT.Identity,
                                      bias=mod[:, 24 * w + k:24 * w + k + 1]).then_inc(src_hi, 1)

            def last_squares(L):
                for g in range(4):
                    act.wait_ge(xT_taken, nth(L, 4, g + 1))
                    squares(2 * g, 2 * g + 2)

            def store_mod(e, i=0):
                if e < N_ADA2:
                    nc_act.activation(mod[:, bass.ds(nth(i, 4, N_ADA1 + e), 1)], acc[:, e % 2, T:T + 1], ACT.Copy)

            def store(L, m, e, dst, i=0):
                chunk_used(act, L, m, i)
                store_mod(e, i)
                nc_act.activation(dst, acc[:, e % 2, 0:T], ACT.Copy).then_inc(acc_free, 1)

            def head_a1(L, u):
                act.wait_ge(d1_done, nth(L, UNITS, u + 1))
                s = st[:, u % 4, :]
                if u < 8:
                    for b in range(2):
                        lo, hi = (0, P) if b == 0 else (P, 384)
                        nc_act.activation(att(u, 1)[:, lo:hi], att(u, 0)[:, lo:hi], ACT.Exp,
                                          bias=s[:, 2 + b:3 + b], accum_out=s[:, 4 + b:5 + b])
                    nc_act.activation(s[:, 6:8], s[:, 2:4], ACT.Exp,
                                      bias=sinks[:, u:u + 1]).then_inc(a1_done, 1)
                else:
                    a.link(nc_act.activation(att(u, 1), att(u, 0), ACT.Abs))
                    a.link(nc_act.activation(att(u, 2), att(u, 1), ACT.Exp, scale=-1.0))
                    nc_act.activation(att(u, 1), att(u, 2), ACT.Ln, bias=one).then_inc(a1_done, 1)

            def head_a2(L, u):
                if u < 8:
                    act.wait_ge(b_done, nth(L, UNITS, u + 1))
                    nc_act.activation(att(u, 2), yac[:, u % 2, 0:384], ACT.Copy).then_inc(a2_done, 1)
                else:
                    act.wait_ge(d3_done, nth(L, 8, u - 8 + 1))
                    nc_act.activation(att(u, 1), att(u, 3), ACT.Exp).then_inc(a2_done, 1)

            def gelu_pair(L, half, c, i):
                m = M_U + half * HALF + c
                e = E_U + (half * HALF + c) // 2
                chunk_used(act, L, m + 1, i)
                nc_act.activation(half_of(half)[:, bass.ds(nth(i, 4 * T, c * T), 2 * T)],
                                  acc[:, e % 2, :], ACT.Gelu).then_inc(acc_free, 1)

            def a_high(L, half, q, i):
                r = half * (HALF // 2) + q
                if q > 1 or not isinstance(i, int) or i:
                    chunk_used(act, L, M_VV + 2 * r - 3, i)
                nc_act.activation(hs[:, 0, q % 2 * 2 * T:(q % 2 + 1) * 2 * T],
                                  half_of(half)[:, bass.ds(nth(i, 4 * T, 2 * q * T), 2 * T)],
                                  ACT.Copy).then_inc(ahi_done, 1)

            act.wait_ge(inputs_in, 80)
            nc_act.activation(cact[:, KD:2 * KD], cact[:, 0:KD], ACT.Silu).then_inc(cact_ready, 1)
            act.wait_ge(angle_done, 1)
            nc_act.activation(sinT[:, :], qk(0), ACT.Sin)
            nc_act.activation(cosT[:, :], qk(1), ACT.Sin).then_inc(rope_table, 1)
            for m in range(AHEAD):
                act_high(act, 0, m)
            with act.Fori(0, depth, 1) as L:
                last_squares(L)
                root(nth(L, 2, 1))
                act.wait_ge(mod_ready, nth(L, 1, 1))
                modulated(L, 0)
                a.clear()
                for c in range(N_QA):
                    act_high(act, L, M_QA + c + AHEAD)
                    store(L, M_QA + c, E_QA + c, qk(c if c < 4 else 12))
                for c in range(N_V):
                    act_high(act, L, M_V + c + AHEAD)
                    store(L, M_V + c, E_V + c, att(c, 1)[:, 0:T])
                for m in range(M_PAD, M_QB):
                    act_high(act, L, m + AHEAD)
                act.preload_act_table_set("natural_log_exp_and_others")
                for s in range(N_QB + N_G + 1):
                    if s < N_QB + N_G:
                        act_high(act, L, M_QB + s + AHEAD)
                    if 1 <= s:
                        c = s - 1
                        dst = qk((8 if c % 2 else 4) + c // 2) if c < N_QB else col(B_GT + (c - N_QB) * T, T)
                        store(L, M_QB + c, E_QB + c, dst)
                    if 1 <= s < UNITS + 1:
                        head_a1(L, s - 1)
                    if 3 <= s < UNITS + 3:
                        head_a2(L, s - 3)
                for k in range(KD):
                    if k == 0:
                        chunk_used(act, L, M_G + N_G - 1)
                    act.wait_ge(y_taken, nth(L, UNITS, LAST_HEAD[k]))
                    nc_act.activation(hs[:, 0, k * T:(k + 1) * T], col(B_Y + k * T, T),
                                      ACT.Copy).then_inc(src_hi, 1)
                a.clear()
                act.preload_act_table(ACT.Sigmoid)
                act.wait_ge(acc_free, nth(L, EVACS, E_WQ + 2))
                with act.Fori(0, N_BR // 4, 1) as i:
                    for c in range(4):
                        both = col(B_GT, 16 * T).rearrange("p (b c t) -> p b c t", b=2, t=T)[
                            :, :, bass.ds(nth(i, 4, c), 1), :].rearrange("p b c t -> p b (c t)")
                        nc_act.activation(both, both, ACT.Sigmoid).then_inc(sig_done, 1)
                        act_high(act, L, M_BR + c + AHEAD, i)
                chunk_used(act, L, M_BR + N_BR - 1)
                for k in range(KD):
                    act.wait_ge(pg_free, nth(L, N_BR + N_OUT, 2 + k + 1))
                    nc_act.activation(hs[:, 0, k * T:(k + 1) * T], col(B_MG + k * T, T),
                                      ACT.Copy).then_inc(src_hi, 1)
                for c in range(N_OUT):
                    act_high(act, L, M_OUT + c + AHEAD)
                    act.wait_ge(pg_free, nth(L, N_BR + N_OUT, 2 + N_BR + c + 1))
                    squares(c, c + 1)
                root(nth(L, 2, 2))
                modulated(L, 1)
                a.clear()
                with act.Fori(0, N_WQ // 4, 1) as i:
                    for c in range(4):
                        act_high(act, L, M_WQ + c + AHEAD, i)
                        store(L, M_WQ + c, E_WQ + c, big[:, bass.ds(nth(i, 4 * T, B_QP + c * T), T)], i)
                for e in range(8):
                    act.wait_ge(sk_done, nth(L, 8, e + 1))
                    nc_act.activation(col(B_SKV + e * 512, 512), acc[:, e % 2, :],
                                      ACT.Copy).then_inc(acc_free, 1)
                act.preload_act_table(ACT.Gelu)
                with act.Fori(0, ITERS, 1) as i:
                    for c in (0, 2):
                        act_high(act, L, M_U + c + AHEAD, i)
                        act_high(act, L, M_U + c + 1 + AHEAD, i)
                        gelu_pair(L, 0, c, i)
                def second_half(i, c):
                    act_high(act, L, M_U + HALF + c + AHEAD, i)
                    act_high(act, L, M_U + HALF + c + 1 + AHEAD, i)
                    gelu_pair(L, 1, c, i)

                second_half(0, 0)
                act.wait_ge(gexp_in, nth(L, 1, 1))
                nc_act.activation(top(K_EXP, 256), top(K_EXP, 256), ACT.Exp).then_inc(gexp_done, 1)
                act.preload_act_table(ACT.Gelu)
                second_half(0, 2)
                act.wait_ge(selT_done, nth(L, 1, 1))
                with act.Fori(1, ITERS, 1) as i:
                    for c in (0, 2):
                        second_half(i, c)

                def values(half, i, last=False):
                    for q in range(2):
                        if not (last and q == 1):
                            a_high(L, half, q + 1, i)
                        for c in (2 * q, 2 * q + 1):
                            act_high(act, L, M_VV + half * HALF + c + AHEAD, i)

                act.wait_ge(mul_done, nth(L, 2 * NG, 2 + NG))
                a_high(L, 0, 0, 0)
                with act.Fori(0, ITERS - 1, 1) as i:
                    values(0, i)
                values(0, ITERS - 1, last=True)
                act.wait_ge(mul_done, nth(L, 2 * NG, 2 + 2 * NG))
                chunk_used(act, L, M_VV + HALF - 3)
                a_high(L, 1, 0, 0)
                with act.Fori(0, ITERS - 1, 1) as i:
                    values(1, i)
                values(1, ITERS - 1, last=True)
                chunk_used(act, L, SPLITS - 1)
                nc_act.activation(col(D, D), yac[:, 2:4, :], ACT.Copy).then_inc(ytok_taken, 1)
                a.clear()
            last_squares(depth)
            root(2 * depth + 1)

        @block.vector
        def _(dve):
            v = nc.vector
            d = Steps(dve, dve_step)
            dve.sem_inc(pg_free, 2)
            dve.sem_inc(mul_done, 2)
            dve.sem_inc(xT_taken, 4)
            dve.sem_inc(ytok_taken, 2)

            def normalised(norm, gain, low=None):
                dve.wait_ge(rms_done, norm)
                d.link(v.reciprocal(rms, rms))
                for k in range(KD + 2):
                    if k < KD:
                        v.scalar_tensor_tensor(col(B_H + k * T, T), x[:, k * T:(k + 1) * T], gain[:, k:k + 1], rms,
                                               ALU.mult, ALU.mult).then_inc(xn_done, 1)
                    if low and k >= 2:
                        low(k - 2)

            def source(L, s, w):
                def low(k):
                    dve.wait_ge(src_hi, nth(L, 4 * KD, s * KD + k + 1))
                    v.scalar_tensor_tensor(hs[:, 1, k * T:(k + 1) * T], col(B_H + k * T, T),
                                           mod[:, 24 * w + k:24 * w + k + 1],
                                           hs[:, 0, k * T:(k + 1) * T].bitcast(F32),
                                           ALU.add, ALU.subtract).then_inc(src_done, 1)
                normalised(nth(L, 2, w + 1), gs[:, w * KD:(w + 1) * KD], low)

            def source_low(L, s, src):
                for k in range(KD):
                    dve.wait_ge(src_hi, nth(L, 4 * KD, s * KD + k + 1))
                    v.tensor_tensor(hs[:, 1, k * T:(k + 1) * T], col(src + k * T, T),
                                    hs[:, 0, k * T:(k + 1) * T].bitcast(F32),
                                    ALU.subtract).then_inc(src_done, 1)

            def rope(L, n):
                c = n if n < 4 else 12
                dve.wait_ge(rot_done, nth(L, 5, n // 2 * 2 + 2 if n < 4 else 5))
                r = pg[:, n // 2, n % 2 * T:(n % 2 + 1) * T] if n < 4 else yac[:, 0, 0:T]
                d.mark(v.tensor_tensor(att(n, 0)[:, 0:T], r, sinT[:, :], ALU.mult))
                d.link(v.tensor_tensor(qk(c), qk(c), cosT[:, :], ALU.mult))
                v.tensor_tensor(qk(c), qk(c), att(n, 0)[:, 0:T], ALU.add).then_inc(rope_done, 1)

            def head_d1(L, u):
                dve.wait_ge(sc_done, nth(L, UNITS, u + 1))
                z, s = pg[:, u % 2, 0:384], st[:, u % 4, :]
                if u < 8:
                    d.link(v.scalar_tensor_tensor(att(u, 0), z, HD ** -0.5, con[:, C_SWB:C_SWB + 384],
                                                  ALU.mult, ALU.add))
                    d.mark(v.tensor_reduce(s[:, 0:1], att(u, 0)[:, 0:P], AX.X, ALU.max))
                    d.link(v.tensor_reduce(s[:, 1:2], att(u, 0)[:, P:384], AX.X, ALU.max))
                    v.tensor_scalar(s[:, 2:4], s[:, 0:2], sinks[:, u:u + 1], -1.0, ALU.max,
                                    ALU.mult).then_inc(d1_done, 1)
                else:
                    v.scalar_tensor_tensor(att(u, 0)[:, 0:T], z[:, 0:T], HD ** -0.5,
                                           con[:, C_SBM:C_SBM + T], ALU.mult, ALU.mult)
                    v.scalar_tensor_tensor(att(u, 0)[:, T:384], z[:, T:384], HD ** -0.5,
                                           con[:, C_SBM:C_SBM + P], ALU.mult, ALU.mult).then_inc(d1_done, 1)

            def masked(dst, src):
                v.tensor_tensor(dst[:, 0:T], src[:, 0:T], con[:, C_SBM:C_SBM + T], ALU.mult)
                return v.tensor_tensor(dst[:, T:384], src[:, T:384], con[:, C_SBM:C_SBM + P], ALU.mult)

            def head_d2(L, u):
                dve.wait_ge(a1_done, nth(L, UNITS, u + 1))
                s = st[:, u % 4, :]
                if u < 8:
                    d.link(v.tensor_tensor(s[:, 8:10], s[:, 4:6], s[:, 6:8], ALU.add))
                    d.link(v.reciprocal(s[:, 10:12], s[:, 8:10]))
                    p = att(u, 1)
                    v.tensor_scalar(p[:, 0:P], p[:, 0:P], s[:, 10:11], None, ALU.mult)
                    v.tensor_scalar(p[:, P:384], p[:, P:384], s[:, 11:12], None,
                                    ALU.mult).then_inc(d2_done, 1)
                else:
                    d.link(v.scalar_tensor_tensor(att(u, 2), att(u, 0), 0.0, att(u, 1), ALU.max, ALU.add))
                    masked(att(u, 3), att(u, 2)).then_inc(d2_done, 1)

            def head_d3(L, u):
                dve.wait_ge(b_done, nth(L, UNITS, u + 1))
                v.tensor_tensor(att(u, 3), att(u, 0), yac[:, u % 2, 0:384], ALU.subtract).then_inc(d3_done, 1)

            def head_d4(L, u):
                dve.wait_ge(a2_done, nth(L, UNITS, u + 1))
                masked(att(u, 2), att(u, 1)).then_inc(d4_done, 1)

            def head_out(L, u):
                dve.wait_ge(av_done, nth(L, UNITS, u + 1))
                h = u - 8
                b, c = (HD * (u // 4), u % 4) if u < 8 else (HD * (h % 2), 4 + h // 2)
                v.tensor_copy(col(B_Y + c * T, T)[b:b + HD, :],
                              yac[b:b + HD, 2 + u % 2, 0:T]).then_inc(y_taken, 1)

            def top16(values, cut, best, index):
                d.link(v.max(best[:, 0:8], values))
                d.mark(v.max_index(index[:, 0:8], best[:, 0:8], values))
                d.link(v.match_replace(cut, best[:, 0:8], values, LOWEST))
                d.link(v.max(best[:, 8:16], cut))
                d.link(v.max_index(index[:, 8:16], best[:, 8:16], cut))

            def subkey_topk(L, i):
                d.link(v.tensor_copy(top(K_CUR, 256), big[:, bass.ds(nth(i, 256, B_SKV), 256)]))
                for p in range(2):
                    top16(top(K_CUR + p * P, P), top(K_CUT, P), top(K_VAL + 16 * p, 16),
                          top(K_REC + 16 * p, 16).bitcast(U32))

            def pair_topk(L, i):
                cand = top(K_CAND, 256)
                shape = [P, 16, 16]
                d.link(v.tensor_tensor(cand.rearrange("p (a b) -> p a b", a=16),
                                       top(K_VAL, 16).unsqueeze(2).to_broadcast(shape),
                                       top(K_VAL + 16, 16).unsqueeze(1).to_broadcast(shape), ALU.add))
                pos_ = top(K_POS, 16).bitcast(U32)
                top16(cand, top(K_CCUT, 256), top(K_BEST8, 16), pos_)
                d.mark(v.tensor_copy(big[:, bass.ds(nth(i, 16, B_TK + K_BEST), 16)], top(K_BEST8, 16)))
                d.mark(v.tensor_scalar(top(K_REC + 32, 16).bitcast(U32), pos_, 4, None, ALU.logical_shift_right))
                d.link(v.tensor_scalar(top(K_REC + 48, 16).bitcast(U32), pos_, 15, None, ALU.bitwise_and))
                v.tensor_copy(big[:, bass.ds(nth(i, 64, B_TK + K_RECS), 64)],
                              top(K_REC, 64).bitcast(U32)).then_inc(topk_done, 1)

            def tokens_of(part, g, i, shape):
                return part[:, bass.ds(nth(i, 2 * GT, g * GT), GT)].unsqueeze(1).to_broadcast(shape)

            def masks(L, half, g, i):
                if half or g or not isinstance(i, int) or i:
                    dve.wait_ge(g_done, nth(L, 4 * NG, 2 * (half * NG + g), i, 4))
                    dve.wait_ge(oh_done, nth(L, 2 * NG, half * NG + g, i, 2))
                v.tensor_tensor(ohi[:, g % 2], iota8[:, :, :], tokens_of(selT[:, 0], g, i, [P, P, GT]), ALU.is_equal)
                d.mark(v.tensor_tensor(eqj[:, :, :], iota8[:, half * HALF:(half + 1) * HALF, :],
                                       tokens_of(selT[:, 1], g, i, [P, HALF, GT]), ALU.is_equal))

            def gate_parts(g, i):
                d.join()
                parts = selg[:, :, bass.ds(nth(i, 2 * GT, g * GT), GT)].unsqueeze(2).to_broadcast([P, GP, HALF, GT])
                v.tensor_tensor(ohj[:, g % 2], eqj[:, :, :].unsqueeze(1).to_broadcast([P, GP, HALF, GT]), parts,
                                ALU.mult).then_inc(oh_done, 1)

            def gate(L, half, g, i):
                dve.wait_ge(g_done, nth(L, 4 * NG, 2 + 2 * (half * NG + g + 1), i, 4))
                dst = half_of(half).rearrange("p (j t) -> p j t", t=T)[
                    :, :, bass.ds(nth(i, 2 * GT, g * GT), GT)]
                v.tensor_tensor(dst, dst, pg[:, g % 2, :].rearrange("p (t j) -> p j t", t=GT),
                                ALU.mult).then_inc(mul_done, 1)

            def chunks_and_gates(L, m, half, i, lag, first=False, last=False):
                for g in range(2):
                    k = g - 2 * lag
                    end = last and g == 1
                    if half and not end:
                        a_low(L, 0, g + 1, i)
                    dve_low(dve, L, m + 2 * g + AHEAD, i)
                    if not end:
                        masks(L, half, k + 1, i)
                    if not (first and g == 0):
                        gate(L, half, k - 1, i)
                    if not end:
                        gate_parts(k + 1, i)
                    dve_low(dve, L, m + 2 * g + 1 + AHEAD, i)

            def a_low(L, half, q, i):
                dve.wait_ge(ahi_done, nth(L, HALF, half * HALF // 2 + q + 1, i, 2))
                s = slice(q % 2 * 2 * T, (q % 2 + 1) * 2 * T)
                v.tensor_tensor(hs[:, 1, s], half_of(half)[:, bass.ds(nth(i, 4 * T, 2 * q * T), 2 * T)],
                                hs[:, 0, s].bitcast(F32), ALU.subtract).then_inc(alo_done, 1)

            dve.wait_ge(inputs_in, 80)
            ang, cang, turns = qk(0), qk(1), qk(2)
            d.link(v.tensor_copy(cang, cosT[:, :].bitcast(I32)))
            d.link(v.tensor_scalar(ang, cang, invf, None, ALU.mult))
            d.link(v.tensor_scalar(turns, ang, 1.0 / (2 * np.pi), None, ALU.mult))
            d.link(v.tensor_scalar(turns, turns, ROUND, None, ALU.add))
            d.link(v.tensor_scalar(turns, turns, ROUND, None, ALU.subtract))
            for part in (TWO_PI_1, TWO_PI_2, TWO_PI_3):
                d.link(v.scalar_tensor_tensor(ang, turns, -part, ang, ALU.mult, ALU.add))
            d.link(v.tensor_scalar(cang, ang, np.pi / 2, None, ALU.add))
            d.link(v.tensor_scalar(turns, cang, np.pi, -2 * np.pi, ALU.is_gt, ALU.mult))
            d.link(v.tensor_tensor(cang, cang, turns, ALU.add))
            v.tensor_scalar(cang, cang, PI_DOWN, -PI_DOWN, ALU.min, ALU.max)
            v.tensor_scalar(ang, ang, PI_DOWN, -PI_DOWN, ALU.min, ALU.max).then_inc(angle_done, 1)
            dve.wait_ge(rope_table, 1)
            d.clear()
            v.tensor_copy(iota8[:, :, :], iota.unsqueeze(2).to_broadcast([P, P, GT]))
            dve.wait_ge(cact_ready, 1)
            for a in range(1, N_ADA1, 2):
                dve.wait_ge(first_ada_in[a // 4], 64)
                w = ada_first(a)
                w3 = w.rearrange("p (k f) -> p k f", k=KD)
                d.link(v.tensor_tensor(w3, w3, cact[:, KD:2 * KD].unsqueeze(2).to_broadcast([P, KD, P]), ALU.mult))
                d.link(v.tensor_tensor(w[:, 0:CH // 2], w[:, 0:CH // 2], w[:, CH // 2:CH], ALU.add))
                v.tensor_tensor(w[:, 0:2 * P], w[:, 0:2 * P], w[:, 2 * P:4 * P], ALU.add).then_inc(first_ada_sums, 1)
            dve.wait_ge(first_ada_done, 1)
            d.link(v.tensor_copy(modn[:, :], yac[:, 0, 0:N_ADA1]))
            d.clear()
            for m in range(AHEAD):
                dve_low(dve, 0, m)
            with dve.Fori(0, depth, 1) as L:
                dve.wait_ge(params_in, nth(L, 16, 16))
                d.link(v.tensor_tensor(mod[:, 0:N_ADA1], modn[:, :], par[:, 0:N_ADA1], ALU.add))
                v.scalar_tensor_tensor(gs[:, 0:KD], mod[:, 8:16], 1.0, par[:, 48:56],
                                       ALU.add, ALU.mult).then_inc(mod_ready, 1)
                source(L, 0, 0)
                d.clear()
                for m in range(M_QB):
                    dve_low(dve, L, m + AHEAD)
                for n in range(5):
                    rope(L, n)
                for c in (0, 2, 4):
                    n = min(2, N_V - c)
                    dve.wait_ge(vT_done, nth(L, N_V, c + n))
                    dst = col(B_VT, TT * 640).rearrange("p (t f) -> p t f", t=TT)
                    for a in range(n):
                        ins = v.tensor_copy(dst[:, :, (c + a) * P:(c + a + 1) * P],
                                            yac[:, 1 + c // 2, a * T:(a + 1) * T].rearrange("p (t f) -> p t f", t=TT))
                    ins.then_inc(vtok_ready, 1)
                for s in range(N_QB + N_G):
                    dve_low(dve, L, M_QB + s + AHEAD)
                    if 1 <= s < UNITS + 1:
                        head_d1(L, s - 1)
                    if 2 <= s < UNITS + 2:
                        head_d2(L, s - 2)
                    if 11 <= s < UNITS + 3:
                        head_d3(L, s - 3)
                    if 12 <= s < UNITS + 4:
                        head_d4(L, s - 4)
                    if 5 <= s < UNITS + 5:
                        head_out(L, s - 5)
                source_low(L, 1, B_Y)
                dve.wait_ge(acc_free, nth(L, EVACS, E_WQ + 2))
                d.link(v.tensor_tensor(mod[:, N_ADA1:48], mod[:, N_ADA1:48], par[:, N_ADA1:48], ALU.add))
                d.link(v.scalar_tensor_tensor(gs[:, KD:2 * KD], mod[:, 32:40], 1.0, par[:, 56:64],
                                              ALU.add, ALU.mult))
                d.clear()
                with dve.Fori(0, N_BR // 4, 1) as i:
                    for c in range(4):
                        dve_low(dve, L, M_BR + c + AHEAD, i)
                        chunk_used(dve, L, M_BR + c, i)
                        dve.wait_ge(sig_done, nth(L, N_BR, c + 1, i, 4))
                        ga = big[:, bass.ds(nth(i, 4 * T, B_GT + c * T), T)]
                        gb = big[:, bass.ds(nth(i, 4 * T, B_GT + (8 + c) * T), T)]
                        d.mark(v.tensor_tensor(ga, ga, pg[:, c % 2, 0:T], ALU.mult))
                        d.link(v.tensor_tensor(gb, gb, pg[:, c % 2, T:2 * T], ALU.mult))
                        v.tensor_tensor(big[:, bass.ds(nth(i, 4 * T, B_MG + c * T), T)], ga, gb,
                                        ALU.add).then_inc(pg_free, 1)
                    d.clear()
                source_low(L, 2, B_MG)
                with dve.Fori(0, N_OUT // 4, 1) as i:
                    for c in range(4):
                        dve_low(dve, L, M_OUT + c + AHEAD, i)
                        chunk_used(dve, L, M_OUT + c, i)
                        xc = x[:, bass.ds(nth(i, 4 * T, c * T), T)]
                        v.scalar_tensor_tensor(xc, pg[:, c % 2, 0:T], mod[:, bass.ds(nth(i, 4, 16 + c), 1)],
                                               xc, ALU.mult, ALU.add).then_inc(pg_free, 1)
                source(L, 3, 1)
                with dve.Fori(0, N_WQ // 4, 1) as i:
                    for c in range(4):
                        dve_low(dve, L, M_WQ + c + AHEAD, i)
                dve.wait_ge(ada_used, nth(L, N_ADA, 2 + N_ADA))
                d.link(v.tensor_copy(modn[:, :], yac[:, 0, 0:N_ADA1]))
                d.clear()
                with dve.Fori(0, ITERS, 1) as i:
                    dve.wait_ge(acc_free, nth(L, EVACS, E_U + 2))
                    for c in range(4):
                        if c == POOL_LOW:
                            dve.wait_ge(pool_low_done, nth(L, ITERS, 1, i, 1))
                            dve.sem_inc(split_done, 1)
                        else:
                            dve_low(dve, L, M_U + c + AHEAD, i)
                        if c == 1:
                            subkey_topk(L, i)
                        if c == 3:
                            pair_topk(L, i)
                    d.clear()
                best = top(K_BEST, 256).rearrange("p (u r) -> p u r", r=16)
                e3 = top(K_EXP, 256).rearrange("p (u r) -> p u r", r=16)
                v.tensor_tensor(e3, best, best[:, :, 0:1].to_broadcast([P, 16, 16]),
                                ALU.subtract).then_inc(gexp_in, 1)
                for c in (0, 1):
                    dve_low(dve, L, M_U + HALF + c + AHEAD)
                dve.wait_ge(gexp_done, nth(L, 1, 1))
                d.link(v.tensor_reduce(top(K_SUM, 16), e3, AX.X, ALU.add))
                d.link(v.reciprocal(top(K_SUM + 16, 16), top(K_SUM, 16)))
                dve_low(dve, L, M_U + HALF + 2 + AHEAD)
                dve.wait_ge(decode_done, nth(L, UNITS, UNITS))
                v.tensor_tensor(top(K_IDX + 512, 256).rearrange("p (u r) -> p u r", r=16), e3,
                                top(K_SUM + 16, 16).unsqueeze(2).to_broadcast([P, 16, 16]),
                                ALU.mult).then_inc(gates_ready, 1)
                dve_low(dve, L, M_U + HALF + 3 + AHEAD)
                dve.wait_ge(selT_done, nth(L, 1, 1))
                gres = top(K_EXP, T)
                for t in range(TT):
                    tok = slice(t * P, (t + 1) * P)
                    v.tensor_copy(selT[:, :, tok], pg[:, t, 0:T].rearrange("p (n t) -> p n t", n=2))
                    d.mark(v.tensor_copy(gres[:, tok], pg[:, t, T:384]))
                for a in range(GP):
                    d.join()
                    d.mark(v.tensor_copy(selg[:, a, :], gres[:, :]))
                    if a < GP - 1:
                        d.join()
                        d.mark(v.tensor_tensor(gres[:, :], gres[:, :], selg[:, a, :], ALU.subtract))
                d.join()
                masks(L, 0, 0, 0)
                gate_parts(0, 0)
                chunks_and_gates(L, M_U + HALF, 0, 1, 1, first=True)
                d.clear()

                with dve.Fori(2, ITERS, 1) as i:
                    chunks_and_gates(L, M_U + HALF, 0, i, 1)
                    d.clear()
                masks(L, 0, 1, ITERS - 1)
                gate(L, 0, -1, ITERS - 1)
                gate_parts(1, ITERS - 1)
                gate(L, 0, 0, ITERS - 1)
                masks(L, 1, 0, 0)
                gate(L, 0, 1, ITERS - 1)
                gate_parts(0, 0)
                a_low(L, 0, 0, 0)
                d.clear()
                chunks_and_gates(L, M_VV, 1, 0, 0, first=True)
                d.clear()
                with dve.Fori(1, ITERS - 1, 1) as i:
                    chunks_and_gates(L, M_VV, 1, i, 0)
                    d.clear()
                chunks_and_gates(L, M_VV, 1, ITERS - 1, 0, last=True)
                gate(L, 1, 1, ITERS - 1)
                a_low(L, 1, 0, 0)
                with dve.Fori(0, ITERS - 1, 1) as i:
                    for q in range(2):
                        a_low(L, 1, q + 1, i)
                        for c in (2 * q, 2 * q + 1):
                            dve_low(dve, L, M_VV + HALF + c + AHEAD, i)
                a_low(L, 1, 1, ITERS - 1)
                for c in range(4):
                    dve_low(dve, L, M_VV + HALF + c + AHEAD, ITERS - 1)
                chunk_used(dve, L, SPLITS - 1)
                v.tensor_copy(col(0, D), yac[:, 0:2, :]).then_inc(ytok_taken, 1)
                for g in range(4):
                    out = acc[:, g, :] if g < 2 else pg[:, g - 2, :]
                    dve.wait_ge(yT_done, nth(L, 4, g + 1))
                    for k in (2 * g, 2 * g + 1):
                        xc = x[:, k * T:(k + 1) * T]
                        ins = v.scalar_tensor_tensor(xc, out[:, k % 2 * T:(k % 2 + 1) * T],
                                                     mod[:, 40 + k:41 + k], xc, ALU.mult, ALU.add)
                    ins.then_inc(xT_taken, 1)
                d.clear()
            normalised(2 * depth + 1, fg)

        @block.gpsimd
        def _(pool):
            g = nc.gpsimd
            s = Steps(pool, pool_step)
            pool.sem_inc(ada_ready, SA)
            with pool.Fori(0, depth, 1) as L:
                with pool.Fori(0, N_ADA // SA, 1) as i:
                    pool.wait_ge(cact_ready, 1)
                    for a in range(SA):
                        pool.wait_ge(ada_in[a], nth(L, N_ADA // SA * 16, 16, i, 16))
                        pool.wait_ge(ada_used, nth(L, N_ADA, a + 1, i, SA))
                        w = adab(a)
                        w3 = w.rearrange("p (k f) -> p k f", k=KD)
                        s.link(g.tensor_tensor(w3, w3, cact[:, KD:2 * KD].unsqueeze(2).to_broadcast([P, KD, P]),
                                               ALU.mult))
                        s.link(g.tensor_tensor(w[:, 0:CH // 2], w[:, 0:CH // 2], w[:, CH // 2:CH], ALU.add))
                        g.tensor_tensor(col(B_RES + a % 2 * 2 * P, 2 * P), w[:, 0:2 * P], w[:, 2 * P:4 * P],
                                        ALU.add).then_inc(ada_ready, 1)
                    s.clear()

                def decode(i):
                    pool.wait_ge(topk_done, nth(L, UNITS, 1, i, 1))
                    rec = big[:, bass.ds(nth(i, 64, B_TK + K_RECS), 64)]
                    eq = top(K_PEQ, 256).rearrange("p (r a) -> p r a", a=16)
                    shape = [P, 16, 16]
                    for p in range(2):
                        s.link(g.tensor_tensor(eq, rec[:, 32 + 16 * p:48 + 16 * p].unsqueeze(2).to_broadcast(shape),
                                               iota16.unsqueeze(1).to_broadcast(shape), ALU.subtract))
                        s.link(g.tensor_scalar(eq, eq, 0.0, None, ALU.is_equal))
                        s.link(g.tensor_tensor(eq, eq, rec[:, 16 * p:16 * p + 16].unsqueeze(1).to_broadcast(shape),
                                               ALU.mult))
                        for n in (8, 4, 2):
                            s.link(g.tensor_tensor(eq[:, :, 0:n], eq[:, :, 0:n], eq[:, :, n:2 * n], ALU.add))
                        s.link(g.tensor_tensor(top(K_PRES + 16 * p, 16).unsqueeze(2), eq[:, :, 0:1], eq[:, :, 1:2],
                                               ALU.add))
                    dst = top(K_IDX, 512).rearrange("p (n c) -> p n c", n=2)[:, :, bass.ds(nth(i, 16, 0), 16)]
                    g.tensor_copy(dst, top(K_PRES, 32).rearrange("p (n c) -> p n c", n=2)).then_inc(decode_done, 1)
                    s.clear()

                def low(i):
                    m = M_U + POOL_LOW + AHEAD
                    pool.wait_ge(hi_done, nth(L, SPLITS, m + 1, i, 4))
                    g.tensor_tensor(wsp[:, m % W, 1, :], raw[:, m % RAW, :], wsp[:, m % W, 0, :].bitcast(F32),
                                    ALU.subtract).then_inc(pool_low_done, 1)

                low(0)
                with pool.Fori(0, UNITS - 1, 1) as i:
                    low(nth(i, 1, 1))
                    decode(i)
                decode(UNITS - 1)

def to_stream(w):
    depth, rows, cols = w.shape
    assert rows == D
    return w.reshape(depth, KD, P, cols // P, P).transpose(0, 3, 2, 1, 4).reshape(depth, cols // P, P, CH)


def kernel(x, c, positions, ada_w, ada_b, norm1_g, w_in, swa_sinks, w_branch_swa, w_branch_sb,
           w_out, norm2_g, peer_wq, peer_subkeys, peer_u, peer_v, final_g):
    import concourse.bacc as bacc
    from concourse.bass_utils import run_bass_kernel_spmd as run

    arr = np.asarray
    x, c, positions = arr(x), arr(c), arr(positions)
    w_in, ada_w, ada_b = arr(w_in), arr(ada_w), arr(ada_b)
    depth = w_in.shape[0]
    f32 = np.float32

    heads = np.arange(8).reshape(2, 4).T.ravel()
    swa_cols = (heads[:, None] * HD + np.arange(HD)[None, :]).ravel()
    off = np.cumsum([0, 512, 128, 128, 512, 512, 512, 1024, 1024])
    qa, ka, va, qb, kb, vb, ga, gb = [np.arange(off[n], off[n + 1]) for n in range(8)]
    order = np.concatenate([qa[swa_cols], ka, va, vb])
    both = np.stack([qb.reshape(4, P), kb.reshape(4, P)], 1).ravel()
    gates = np.concatenate([ga, gb])

    def columns(v, n):
        return arr(v).reshape(depth, n, P).transpose(0, 2, 1)

    params = np.zeros((depth, P, 72), f32)
    params[:, :, 0:48] = columns(ada_b, 48)
    params[:, :, 48:56] = columns(norm1_g, KD)
    params[:, :, 56:64] = columns(norm2_g, KD)
    params[:, :, 64:72] = arr(swa_sinks)[:, None, :]
    sub = arr(peer_subkeys).reshape(depth, 2, 8, P, P).transpose(0, 1, 4, 2, 3)
    sub = np.ascontiguousarray(sub.reshape(depth, 2, P, CH).transpose(0, 2, 1, 3)).reshape(depth, P, 2 * CH)
    ada = np.zeros((depth * N_ADA + N_ADA1, P, CH), f32)
    ada[:depth * N_ADA] = to_stream(ada_w).reshape(-1, P, CH)
    whole = np.zeros((depth * SPLITS + RAW, P, CH), f32)
    stream = whole[:depth * SPLITS].reshape(depth, SPLITS, P, CH)
    branch = np.concatenate([arr(w_branch_swa)[:, swa_cols], arr(w_branch_sb)], 1)
    for m, w in ((M_QA, w_in[:, :, order]), (M_QB, w_in[:, :, both]), (M_G, w_in[:, :, gates]), (M_BR, branch),
                 (M_OUT, arr(w_out)), (M_WQ, arr(peer_wq))):
        s = to_stream(w)
        stream[:, m:m + s.shape[1]] = s
    u = arr(peer_u).reshape(depth, P, P, KD, P)
    stream[:, M_U:M_VV] = u.transpose(0, 2, 4, 3, 1).reshape(depth, N_U, P, CH)
    stream[:, M_VV:] = arr(peer_v).reshape(depth, P, P, D).transpose(0, 2, 1, 3)

    arrays = {
        "consts": constants(),
        "stream": whole,
        "ada": ada,
        "subkeys": sub,
        "params": params,
        "xT": np.ascontiguousarray(x[0].reshape(T, KD, P).transpose(2, 1, 0).reshape(P, KD * T)),
        "cT": np.ascontiguousarray(c[0].reshape(KD, P).T),
        "pos": np.ascontiguousarray(np.broadcast_to(positions, (P, T))).astype(np.int32),
        "final_g": np.ascontiguousarray(arr(final_g).reshape(KD, P).T),
    }
    nc = bacc.Bacc("TRN2", target_bir_lowering=False, num_devices=1, dynamic_dma_scratch_size=64)
    aps = [nc.dram_tensor(k, v.shape, mybir.dt.from_np(v.dtype), kind="ExternalInput").ap()
           for k, v in arrays.items()]
    out = nc.dram_tensor("outT", (P, KD * T), F32, kind="ExternalOutput").ap()
    build(nc, depth, *aps, out)
    got = run(nc, [arrays], core_ids=[0]).results[0]["outT"]
    return got.reshape(P, KD, T).transpose(2, 1, 0).reshape(1, T, D)
```
